# Optimizing a Trainium2 kernel written in Bass

```python
import jax, jax.numpy as jnp
from jax import lax
import numpy as np

D_MODEL = 1024
BATCH = 1
SEQ = 512
DEPTH = 2
DEC_BATCH = 8
DEC_SEQ = 4
PAST_LEN = 512
PAGE_SIZE = 128

N_MIXERS = 2
N_CONV_LAYERS = (DEPTH + 1) // 2
N_SB_LAYERS = DEPTH // 2
CONV_WIDTH = 31
N_HEADS = 16
HEAD_DIM = D_MODEL // N_HEADS
Q_BLOCK = 128
N_GROUPS = 4
EXPERTS_PER_GROUP = 8
N_EXPERTS = N_GROUPS * EXPERTS_PER_GROUP
TOP_K_FINE = 2
D_EXPERT = D_MODEL // 4
NORM_EPS = 1e-6
LN_EPS = 1e-5
SB_BIAS_INIT = -6.0

kernel_name = "hybrid_conformer_conv_stickbreaking_hmoe_step"

def rmsnorm(x, g):
    xf = x.astype(jnp.float32)
    y = xf * lax.rsqrt(jnp.mean(xf * xf, axis=-1, keepdims=True) + NORM_EPS)
    return (y * g.astype(jnp.float32)).astype(x.dtype)

def layernorm(x, g, b):
    xf = x.astype(jnp.float32)
    mu = jnp.mean(xf, axis=-1, keepdims=True)
    xc = xf - mu
    var = jnp.mean(xc * xc, axis=-1, keepdims=True)
    y = xc * lax.rsqrt(var + LN_EPS) * g.astype(jnp.float32) + b.astype(jnp.float32)
    return y.astype(x.dtype)

def conv_module(x, hist, w_pw1, b_pw1, w_dw, b_dw, ln_g, ln_b, w_pw2, b_pw2):
    a = x @ w_pw1 + b_pw1
    u = a[..., :D_MODEL] * jax.nn.sigmoid(a[..., D_MODEL:])
    full = jnp.concatenate([hist.astype(u.dtype), u], axis=1)
    c = lax.conv_general_dilated(full, w_dw[:, None, :], window_strides=(1,), padding='VALID',
                                 dimension_numbers=('NWC', 'WIO', 'NWC'),
                                 feature_group_count=D_MODEL) + b_dw
    c = jax.nn.silu(layernorm(c, ln_g, ln_b))
    y = c @ w_pw2 + b_pw2
    return y, full[:, -(CONV_WIDTH - 1):]

def stick_breaking(q, k, v, q_pos, k_pos, bias):
    z = jnp.einsum('bqhd,bkhd->bhqk', q, k).astype(jnp.float32) * (HEAD_DIM ** -0.5)
    z = z + bias.astype(jnp.float32)[None, :, None, None]
    mask = k_pos[None, :] < q_pos[:, None]
    log_fail = jnp.where(mask, jax.nn.log_sigmoid(-z), 0.0)
    between = lax.cumsum(log_fail, axis=3, reverse=True) - log_fail
    attn = jnp.where(mask, jnp.exp(jax.nn.log_sigmoid(z) + between), 0.0)
    return jnp.einsum('bhqk,bkhd->bqhd', attn.astype(v.dtype), v)

def qkv_proj(x, w_qkv):
    B, T, _ = x.shape
    qkv = (x @ w_qkv).reshape(B, T, 3, N_HEADS, HEAD_DIM)
    return qkv[:, :, 0], qkv[:, :, 1], qkv[:, :, 2]

def sb_prompt(x, w_qkv, w_o, bias):
    B, T, _ = x.shape
    q, k, v = qkv_proj(x, w_qkv)
    nb = T // Q_BLOCK
    pos = jnp.arange(T, dtype=jnp.int32)
    qb = q.reshape(B, nb, Q_BLOCK, N_HEADS, HEAD_DIM).transpose(1, 0, 2, 3, 4)
    pb = pos.reshape(nb, Q_BLOCK)
    ob = lax.map(lambda a: stick_breaking(a[0], k, v, a[1], pos, bias), (qb, pb))
    o = ob.transpose(1, 0, 2, 3, 4).reshape(B, T, D_MODEL)
    return o @ w_o, k, v

def sb_sample(x, cache_k, cache_v, page_table, w_qkv, w_o, bias):
    B, T, _ = x.shape
    q, k, v = qkv_proj(x, w_qkv)
    past = page_table.shape[1] * PAGE_SIZE
    k_past = cache_k[page_table].reshape(B, past, N_HEADS, HEAD_DIM)
    v_past = cache_v[page_table].reshape(B, past, N_HEADS, HEAD_DIM)
    k_all = jnp.concatenate([k_past.astype(k.dtype), k], axis=1)
    v_all = jnp.concatenate([v_past.astype(v.dtype), v], axis=1)
    q_pos = past + jnp.arange(T, dtype=jnp.int32)
    k_pos = jnp.arange(past + T, dtype=jnp.int32)
    o = stick_breaking(q, k_all, v_all, q_pos, k_pos, bias).reshape(B, T, D_MODEL)
    return o @ w_o, k, v

def hier_moe(x, w_coarse, b_coarse, w_fine, b_fine, w_gate, w_up, w_down):
    B, T, _ = x.shape
    xt = x.reshape(B * T, D_MODEL)
    coarse = (xt @ w_coarse).astype(jnp.float32) + b_coarse.astype(jnp.float32)
    p_group = jax.nn.softmax(coarse, axis=-1)
    g_top, g_idx = lax.top_k(p_group, 1)
    fine_all = jnp.einsum('nd,gde->nge', xt, w_fine).astype(jnp.float32) + b_fine.astype(jnp.float32)
    fine = jnp.take_along_axis(fine_all, g_idx[:, :, None], axis=1)[:, 0]
    p_exp = jax.nn.softmax(fine, axis=-1)
    e_top, e_idx = lax.top_k(p_exp, TOP_K_FINE)
    e_w = e_top / jnp.sum(e_top, axis=-1, keepdims=True)
    within = jnp.sum(jax.nn.one_hot(e_idx, EXPERTS_PER_GROUP, dtype=jnp.float32) * e_w[..., None], axis=1)
    comb = jax.nn.one_hot(g_idx[:, 0], N_GROUPS, dtype=jnp.float32)[:, :, None] * (g_top * within)[:, None, :]
    comb = comb.reshape(B * T, N_EXPERTS).astype(x.dtype)
    h = jax.nn.silu(jnp.einsum('nd,edf->nef', xt, w_gate)) * jnp.einsum('nd,edf->nef', xt, w_up)
    y = jnp.einsum('nef,efd->nd', h * comb[:, :, None], w_down)
    return y.reshape(B, T, D_MODEL)

def setup_inputs(seed: int = 0) -> dict:
    key = jax.random.key(seed)
    ks = jax.random.split(key, 32)
    f32 = jnp.float32

    def nrm(k, shape, scale):
        return jax.random.normal(k, shape, f32) * scale

    n_pages = PAST_LEN // PAGE_SIZE
    n_used = DEC_BATCH * n_pages
    n_pool = n_used + n_used // 4
    perm = jax.random.permutation(ks[5], n_pool)
    page_table = perm[:n_used].reshape(DEC_BATCH, n_pages).astype(jnp.int32)
    D = D_MODEL
    return {
        "x_prompt": nrm(ks[0], (BATCH, SEQ, D), 1.0),
        "x_sample": nrm(ks[1], (DEC_BATCH, DEC_SEQ, D), 1.0),
        "state_conv": nrm(ks[2], (N_CONV_LAYERS, DEC_BATCH, CONV_WIDTH - 1, D), 1.0),
        "cache_k": nrm(ks[3], (N_SB_LAYERS, n_pool, PAGE_SIZE, N_HEADS, HEAD_DIM), 1.0),
        "cache_v": nrm(ks[4], (N_SB_LAYERS, n_pool, PAGE_SIZE, N_HEADS, HEAD_DIM), 1.0),
        "page_table": page_table,
        "norm_mix": 1.0 + nrm(ks[6], (DEPTH, D), 0.05),
        "norm_ffn": 1.0 + nrm(ks[7], (DEPTH, D), 0.05),
        "norm_final": 1.0 + nrm(ks[8], (D,), 0.05),
        "conv_w_pw1": nrm(ks[9], (N_CONV_LAYERS, D, 2 * D), D ** -0.5),
        "conv_b_pw1": nrm(ks[10], (N_CONV_LAYERS, 2 * D), 0.02),
        "conv_w_dw": nrm(ks[11], (N_CONV_LAYERS, CONV_WIDTH, D), CONV_WIDTH ** -0.5),
        "conv_b_dw": nrm(ks[12], (N_CONV_LAYERS, D), 0.02),
        "conv_ln_g": 1.0 + nrm(ks[13], (N_CONV_LAYERS, D), 0.05),
        "conv_ln_b": nrm(ks[14], (N_CONV_LAYERS, D), 0.02),
        "conv_w_pw2": nrm(ks[15], (N_CONV_LAYERS, D, D), D ** -0.5),
        "conv_b_pw2": nrm(ks[16], (N_CONV_LAYERS, D), 0.02),
        "sb_w_qkv": nrm(ks[17], (N_SB_LAYERS, D, 3 * D), D ** -0.5),
        "sb_w_o": nrm(ks[18], (N_SB_LAYERS, D, D), D ** -0.5),
        "sb_logit_bias": SB_BIAS_INIT + nrm(ks[26], (N_SB_LAYERS, N_HEADS), 0.1),
        "moe_w_coarse": nrm(ks[19], (DEPTH, D, N_GROUPS), D ** -0.5),
        "moe_b_coarse": nrm(ks[20], (DEPTH, N_GROUPS), 0.01),
        "moe_w_fine": nrm(ks[21], (DEPTH, N_GROUPS, D, EXPERTS_PER_GROUP), D ** -0.5),
        "moe_b_fine": nrm(ks[22], (DEPTH, N_GROUPS, EXPERTS_PER_GROUP), 0.01),
        "moe_w_gate": nrm(ks[23], (DEPTH, N_EXPERTS, D, D_EXPERT), D ** -0.5),
        "moe_w_up": nrm(ks[24], (DEPTH, N_EXPERTS, D, D_EXPERT), D ** -0.5),
        "moe_w_down": nrm(ks[25], (DEPTH, N_EXPERTS, D_EXPERT, D), D_EXPERT ** -0.5),
    }

def reference(x_prompt, x_sample, state_conv, cache_k, cache_v, page_table, norm_mix, norm_ffn, norm_final,
              conv_w_pw1, conv_b_pw1, conv_w_dw, conv_b_dw, conv_ln_g, conv_ln_b, conv_w_pw2, conv_b_pw2,
              sb_w_qkv, sb_w_o, sb_logit_bias, moe_w_coarse, moe_b_coarse, moe_w_fine, moe_b_fine,
              moe_w_gate, moe_w_up, moe_w_down):
    yp, ys = x_prompt, x_sample
    conv_p, conv_s, k_p, v_p, k_s, v_s = [], [], [], [], [], []
    for i in range(DEPTH):
        j = i // N_MIXERS
        hp = rmsnorm(yp, norm_mix[i])
        hs = rmsnorm(ys, norm_mix[i])
        if i % N_MIXERS == 0:
            cw = (conv_w_pw1[j], conv_b_pw1[j], conv_w_dw[j], conv_b_dw[j],
                  conv_ln_g[j], conv_ln_b[j], conv_w_pw2[j], conv_b_pw2[j])
            zero_hist = jnp.zeros((hp.shape[0], CONV_WIDTH - 1, D_MODEL), hp.dtype)
            mp, sp = conv_module(hp, zero_hist, *cw)
            ms, ss = conv_module(hs, state_conv[j], *cw)
            conv_p.append(sp)
            conv_s.append(ss)
        else:
            mp, kp_new, vp_new = sb_prompt(hp, sb_w_qkv[j], sb_w_o[j], sb_logit_bias[j])
            ms, ks_new, vs_new = sb_sample(hs, cache_k[j], cache_v[j], page_table, sb_w_qkv[j], sb_w_o[j],
                                           sb_logit_bias[j])
            k_p.append(kp_new)
            v_p.append(vp_new)
            k_s.append(ks_new)
            v_s.append(vs_new)
        yp = yp + mp
        ys = ys + ms
        mw = (moe_w_coarse[i], moe_b_coarse[i], moe_w_fine[i], moe_b_fine[i],
              moe_w_gate[i], moe_w_up[i], moe_w_down[i])
        yp = yp + hier_moe(rmsnorm(yp, norm_ffn[i]), *mw)
        ys = ys + hier_moe(rmsnorm(ys, norm_ffn[i]), *mw)
    yp = rmsnorm(yp, norm_final)
    ys = rmsnorm(ys, norm_final)
    return (yp, ys, jnp.stack(conv_p), jnp.stack(conv_s), jnp.stack(k_p), jnp.stack(v_p),
            jnp.stack(k_s), jnp.stack(v_s))


_drawn_inputs = setup_inputs


def setup_inputs(seed=0):
    import zlib

    import numpy as np

    out = dict(_drawn_inputs(seed))
    spreads = {}
    factors = {'sb_logit_bias': 31.688,
     'moe_b_coarse': 4.832,
     'moe_b_fine': 3.698,
     'cache_k': 8.0,
     'cache_v': 8.0,
     'sb_w_o': 8.0}
    for name, (base, spread) in spreads.items():
        noise = np.random.default_rng([zlib.crc32(name.encode()), seed]).standard_normal(out[name].shape)
        drawn = base * np.exp(spread * noise) if base else spread * noise
        out[name] = __import__('jax').numpy.asarray(drawn.astype(out[name].dtype))
    for name, factor in factors.items():
        out[name] = (out[name] * factor).astype(out[name].dtype)
    return out
```

```python
import concourse.bass as bass
from concourse import mybir
import numpy as np
from contextlib import ExitStack

F32 = mybir.dt.float32
BF16 = mybir.dt.bfloat16
I32 = mybir.dt.int32
U32 = mybir.dt.uint32
ALU = mybir.AluOpType
ACT = mybir.ActivationFunctionType
AX = mybir.AxisListType

P = 128
D = 1024
KT = D // P
SEQ = 512
DB, DS = 8, 4
NS = DB * DS
TOK = SEQ + NS
NB = SEQ // P + 1
ROWS = [P] * (SEQ // P) + [NS]
HALF = TOK // 2
W = 31
POOLT = 9
HIST = W - 1
STREAM = HIST + SEQ + DB * (HIST + DS)
SAMPLE0 = HIST + SEQ
NH, DH = 16, 64
PAST, PAGE = 512, 128
NPG = PAST // PAGE
NG, EPG = 4, 8
NE = NG * EPG
NR = NG + NE
FE = D // 4
SLOTS = 2 * TOK
CAP = 96
NPASS = -(-TOK // CAP)
XCOLS = SLOTS + CAP
RING = 4
NORM_EPS, LN_EPS = 1e-6, 1e-5
NEG = -1.0e30
V_DW, V_MIX, V_FFN, V_B1, V_BDW, V_LNG, V_LNB, NV = 0, 31, 33, 35, 37, 38, 39, 40
A_HN = 0
A_HT = A_HN + NB * D
A_XS = A_HT + KT * TOK
A_RING = A_XS + KT * XCOLS
EW = 3 * KT * FE
A_END = A_RING + RING * EW
PIECE = 384
PIECES = [(o, min(PIECE, SLOTS - o)) for o in range(0, SLOTS, PIECE)]
A_PART = A_RING + 2 * EW
A_PICK = A_PART + 3 * NB * D // 2
A_COUNT = A_HT


class Chain:

    def __init__(self, eng, sem):
        self.eng, self.sem, self.n = eng, sem, 0

    def __call__(self, ins):
        self.n += 1
        ins.then_inc(self.sem, 1)
        self.eng.wait_ge(self.sem, self.n)


class LoopChain:

    def __init__(self, eng, sem, it, per):
        self.eng, self.sem, self.it, self.per, self.n = eng, sem, it, per, 0

    def __call__(self, ins):
        self.n += 1
        assert self.n <= self.per
        ins.then_inc(self.sem, 1)
        self.eng.wait_ge(self.sem, self.it * self.per + self.n)


class Kernel:

    def __init__(self, nc, ctx, dram):
        self.nc, self.ctx, self.d = nc, ctx, dram
        self.sems = []
        self.settled = nc.alloc_semaphore(name="waits_carried")
        self.X = self.sb("X", [P, NB, D])
        self.arena = self.sb("arena", [P, A_END])
        self.ident = self.sb("ident", [P, P])
        self.before = self.sb("before", [P, P])
        self.negtri = self.sb("negtri", [P, P])
        self.ones = self.sb("ones", [P, P])
        self.negones = self.sb("negones", [P, P])
        self.iota = self.sb("iota", [P, NE])
        self.valid = self.sb("valid", [P, NB])
        self.vec = self.sb("vec", [P, KT, NV])
        self.wr = self.sb("wr", [P, 2, KT, NR])
        self.br = self.sb("br", [P, 2, NR])
        self.ss = self.sb("ss", [P, NB])
        self.rstd = self.sb("rstd", [P, NB])
        self.wts = self.sb("wts", [P, NB, 2])
        self.pos = self.sb("pos", [P, NB, 2], I32)
        self.posf = self.sb("posf", [P, NB, 2])
        self.start = self.sb("start", [P, NE], I32)
        self.starts = self.sb("starts", [P, NE * NPASS], I32)
        self.over = self.sb("over", [P, 1], I32)
        self.psum = ctx.enter_context(nc.psum_tensor("psum", [P, 8 * 512], F32))
        self.ps = [self.psum[:, 512 * i:512 * i + 512] for i in range(8)]
        self.ys_dram = nc.dram_tensor("slots_out", [XCOLS, D], F32, kind="Internal").ap()

    def sb(self, name, shape, dt=F32):
        return self.ctx.enter_context(self.nc.sbuf_tensor(name, shape, dt))

    def sem(self, name):
        self.sems.append(self.nc.alloc_semaphore(name=name))
        return self.sems[-1]

    def settle(self, eng):
        eng.sem_inc(self.settled, 1)

    def recycle(self):
        self.nc.clear_and_free_semaphores(self.sems)
        self.nc.all_engine_barrier()
        self.sems = []

    def region(self, at, *dims):
        n = 1
        for x in dims:
            n *= x
        assert at + n <= A_END
        v = self.arena[:, at:at + n]
        if len(dims) == 1:
            return v
        names = "abcd"[:len(dims)]
        return v.rearrange(f"p ({' '.join(names)}) -> p {' '.join(names)}", **dict(zip(names[1:], dims[1:])))

    def HN(self):
        return self.region(A_HN, NB, D)

    def region16(self, at, *dims):
        n = int(np.prod(dims))
        v = self.arena[:, at:at + n // 2].bitcast(BF16)
        return v.rearrange("p (a b) -> p a b", b=dims[1])

    def part(self, i):
        return self.region16(A_PART + i * NB * D // 2, NB, D)

    def HT(self):
        return self.region(A_HT, KT, TOK)


def stage_setup(K):
    nc, d = K.nc, K.d
    s_vec, s_x, s_c, s_t, s_v = (K.sem(f"setup_{n}") for n in ("vec", "x", "const", "turn", "out"))
    s_pool, s_br = K.sem("setup_pool"), K.sem("setup_br")
    rows = K.region(A_RING, D)

    with nc.Block() as block:
        @block.sync
        def _(sp):
            sp.dma_start(rows[V_DW:V_DW + W], d["conv_w_dw"][0]).then_inc(s_vec, 16)
            sp.dma_start(rows[V_MIX:V_MIX + 2], d["norm_mix"]).then_inc(s_vec, 16)
            sp.dma_start(rows[V_FFN:V_FFN + 2], d["norm_ffn"]).then_inc(s_vec, 16)
            sp.dma_start(rows[V_B1:V_B1 + 2], d["conv_b_pw1"].rearrange("a (h c) -> (a h) c", h=2)).then_inc(s_vec, 16)
            for r, n in ((V_BDW, "conv_b_dw"), (V_LNG, "conv_ln_g"), (V_LNB, "conv_ln_b")):
                sp.dma_start(rows[r:r + 1], d[n]).then_inc(s_vec, 16)
            sp.dma_start(K.X[:, 0:4, :], d["x_prompt"][0].rearrange("(b p) c -> p b c", p=P)).then_inc(s_x, 16)
            sp.dma_start(K.X[0:NS, 4, :], d["x_sample"].rearrange("s t c -> (s t) c")).then_inc(s_x, 16)
            sp.wait_ge(s_x, 32)

        @block.scalar
        def _(act):
            for i in range(2):
                act.dma_start(K.wr[:, i, :, 0:NG], d["moe_w_coarse"][i].rearrange("(k p) g -> p k g", p=P)).then_inc(s_br, 16)
                for g in range(NG):
                    act.dma_start(K.wr[:, i, :, NG + EPG * g:NG + EPG * (g + 1)],
                                  d["moe_w_fine"][i, g].rearrange("(k p) e -> p k e", p=P)).then_inc(s_br, 16)
                act.dma_start(K.br[:, i, 0:NG], d["moe_b_coarse"][i:i + 1, :].partition_broadcast(P)).then_inc(s_br, 16)
                act.dma_start(K.br[:, i, NG:NR], d["moe_b_fine"][i:i + 1].rearrange("a g e -> a (g e)").partition_broadcast(P)).then_inc(s_br, 16)
            act.wait_ge(s_br, 16 * 2 * (NG + 3))

        @block.gpsimd
        def _(pool):
            chain = Chain(pool, s_pool)
            nc.gpsimd.memset(K.ident[:], 0.0)
            nc.gpsimd.memset(K.before[:], 0.0)
            nc.gpsimd.memset(K.negtri[:], 0.0)
            nc.gpsimd.memset(K.ones[:], 1.0)
            nc.gpsimd.memset(K.negones[:], -1.0)
            chain(nc.gpsimd.memset(K.valid[:], 1.0))
            nc.gpsimd.affine_select(out=K.ident[:], in_=K.ident[:], compare_op=ALU.not_equal, fill=1.0, base=0,
                                    pattern=[[-1, P]], channel_multiplier=1).then_inc(s_c, 1)
            nc.gpsimd.affine_select(out=K.before[:], in_=K.before[:], compare_op=ALU.is_ge, fill=1.0, base=0,
                                    pattern=[[-1, P]], channel_multiplier=1)
            nc.gpsimd.affine_select(out=K.negtri[:], in_=K.negtri[:], compare_op=ALU.is_gt, fill=-1.0, base=0,
                                    pattern=[[1, P]], channel_multiplier=-1)
            nc.gpsimd.affine_select(out=K.valid[:], in_=K.valid[:], compare_op=ALU.is_gt, fill=0.0,
                                    base=NS + P * (NB - 1), pattern=[[-P, NB]], channel_multiplier=-1)
            nc.gpsimd.iota(K.iota[:], pattern=[[1, NE]], base=0, channel_multiplier=0,
                           allow_small_or_imprecise_dtypes=True)

        @block.vector
        def _(dve):
            nc.vector.memset(K.ss[:], 1.0)
            for k in range(KT):
                dve.wait_ge(s_t, k + 1)
                nc.vector.tensor_copy(K.vec[:, k, :], K.ps[k][:, 0:NV])

        @block.tensor
        def _(pe):
            pe.wait_ge(s_c, 1)
            pe.wait_ge(s_vec, 7 * 16)
            for k in range(KT):
                nc.tensor.transpose(K.ps[k][:, 0:NV], rows[0:NV, k * P:(k + 1) * P], K.ident[0:NV, 0:NV]).then_inc(s_t, 1)


def stage_norm(K, tag, gain_row):
    nc = K.nc
    s_sq, s_ms, s_rt, s_rs, s_hn, s_t, s_e = (
        K.sem(f"{tag}_{n}") for n in ("squares", "mean", "root", "rstd", "scaled", "turned", "out"))
    HN, HT = K.HN(), K.HT()
    small = K.ps[7][:, 0:KT * NS].rearrange("p (k t) -> p k t", k=KT)

    with nc.Block() as block:
        @block.scalar
        def _(act):
            for b, r in enumerate(ROWS):
                nc.scalar.activation(HN[0:r, b, :], K.X[0:r, b, :], ACT.Square, accum_out=K.ss[0:r, b:b + 1]).then_inc(s_sq, 1)
            act.wait_ge(s_ms, 1)
            nc.scalar.activation(K.rstd[:], K.ss[:], ACT.Sqrt).then_inc(s_rt, 1)
            act.wait_ge(s_rs, 1)
            for b in (1, 3):
                nc.scalar.activation(HN[:, b, :], K.X[:, b, :], ACT.Copy, scale=K.rstd[:, b:b + 1]).then_inc(s_hn, 1)
            for k in range(1, KT, 2):
                act.wait_ge(s_t, k + 1)
                nc.scalar.activation(HT[:, k, 0:SEQ], K.ps[k % 6][:], ACT.Copy, scale=K.vec[:, k, gain_row:gain_row + 1]).then_inc(s_e, 1)

        @block.vector
        def _(dve):
            dve.wait_ge(s_sq, NB)
            nc.vector.tensor_scalar(K.ss[:], K.ss[:], 1.0 / D, NORM_EPS, ALU.mult, ALU.add).then_inc(s_ms, 1)
            dve.wait_ge(s_rt, 1)
            nc.vector.reciprocal(K.rstd[:], K.rstd[:]).then_inc(s_rs, 1)
            dve.wait_ge(s_rs, 1)
            for b in (0, 2, 4):
                r = ROWS[b]
                nc.vector.tensor_scalar(HN[0:r, b, :], K.X[0:r, b, :], K.rstd[0:r, b:b + 1], None, ALU.mult).then_inc(s_hn, 1)
            for k in range(0, KT, 2):
                dve.wait_ge(s_t, k + 1)
                nc.vector.tensor_scalar(HT[:, k, 0:SEQ], K.ps[k % 6][:], K.vec[:, k, gain_row:gain_row + 1], None, ALU.mult).then_inc(s_e, 1)
            dve.wait_ge(s_t, KT)
            nc.vector.tensor_tensor(HT[:, :, SEQ:TOK], small, K.vec[:, :, gain_row:gain_row + 1].to_broadcast([P, KT, NS]), ALU.mult)

        @block.tensor
        def _(pe):
            pe.wait_ge(s_hn, NB)
            for k in range(KT):
                if k >= 6:
                    pe.wait_ge(s_e, KT - 2)
                cols = slice(k * P, (k + 1) * P)
                nc.tensor.transpose(small[:, k, :], HN[0:NS, NB - 1, cols], K.ident[0:NS, 0:NS])
                for b in range(4):
                    last = nc.tensor.transpose(K.ps[k % 6][:, b * P:(b + 1) * P], HN[:, b, cols], K.ident[:])
                last.then_inc(s_t, 1)


def stage_conv_in(K):
    nc, d = K.nc, K.d
    names = ("hist", "histT", "histout", "proj", "sig", "glu", "gchain", "tap", "zero", "prod", "added", "sprod", "sred", "merged")
    s = {n: K.sem(f"conv_{n}") for n in names}
    s_w = [K.sem(f"conv_w{u}") for u in range(2)]
    s_st = K.sem("conv_state_rows")
    s_tr, s_ev, s_out = K.sem("conv_tail_turned"), K.sem("conv_tail_out"), K.sem("conv_state_stored")
    HT = K.HT()
    at = A_XS
    U = K.region(at, KT, STREAM); at += KT * STREAM
    C = K.region(at, KT, TOK); at += KT * TOK
    wt = [K.region(at + u * KT * 2 * P, KT, 2, P) for u in range(2)]; at += 2 * KT * 2 * P
    sg = [K.region(at + u * TOK, TOK) for u in range(2)]; at += 2 * TOK
    hist = K.region(at, 2, D); at += 2 * D
    tail = K.region(at, 2, D); at += 2 * D
    fresh = K.region(at, KT, NS); at += KT * NS
    hn = A_HN
    prods = [K.region(hn + i * SEQ, SEQ) for i in range(3)]; hn += 3 * SEQ
    psum_p = [K.region(hn + i * SEQ, SEQ) for i in range(2)]; hn += 2 * SEQ
    C2 = K.region(hn, SEQ); hn += SEQ
    sprod = K.region(hn, DB, DS, W); hn += DB * DS * W
    sred = [K.region(hn + i * NS, DB, DS, 1) for i in range(2)]; hn += 2 * NS
    assert hn <= A_HT and POOLT % 3 == 0
    K.C = C
    K.w2 = K.region(at, KT, D); at += KT * D
    K.conv_end = at
    K.s_w2 = K.sem("conv_w_pw2")
    wsrc = d["conv_w_pw1"][0].rearrange("(k p) (h c m) -> c p k h m", p=P, h=2, m=P)
    NHR = DB // 2 * HIST
    loops = KT // 2

    def stream(ct, lo, hi):
        return U[:, ct, lo:hi]

    def samples(ct, lo, n):
        return U[:, ct, SAMPLE0:STREAM].rearrange("p (s t) -> p s t", t=HIST + DS)[:, :, lo:lo + n]

    with nc.Block() as block:
        @block.sync
        def _(sp):
            sp.dma_start(hist[0:NHR], d["state_conv"][0].rearrange("(a s) t c -> (s t) a c", a=2)).then_inc(s["hist"], 16)
            sp.dma_start(d["conv_state_s"][0, :, 0:HIST - DS, :], d["state_conv"][0, :, DS:HIST, :]).then_inc(s_st, 16)
            with sp.Fori(0, loops) as it:
                for u in range(2):
                    sp.wait_ge(s["proj"], 2 * it + u + 1)
                    sp.dma_start(wt[u][:, :, 0, :], wsrc[2 * it + u][:, :, 0, :]).then_inc(s_w[u], 16)
                    sp.dma_start(wt[u][:, :, 1, :], wsrc[2 * it + u][:, :, 1, :]).then_inc(s_w[u], 16)
            sp.dma_start(K.w2, d["conv_w_pw2"][0].rearrange("(k p) c -> p k c", p=P)).then_inc(K.s_w2, 16)
            sp.wait_ge(s_st, 16)
            sp.wait_ge(s_ev, 4)
            sp.dma_start(d["conv_state_p"][0, 0], tail[0:HIST, 0, :]).then_inc(s_out, 16)
            for q in range(DB):
                sp.dma_start(d["conv_state_s"][0, q, HIST - DS:HIST, :], tail[DS * q:DS * (q + 1), 1, :]).then_inc(s_out, 16)
            sp.wait_ge(s_out, 16 * (1 + DB))

        @block.gpsimd
        def _(pool):
            nc.gpsimd.memset(U[:, :, 0:HIST], 0.0).then_inc(s["zero"], 1)
            pool.sem_inc(s["added"], POOLT - 1)
            with pool.Fori(0, loops) as it:
                for u in range(2):
                    ct = 2 * it + u
                    pool.wait_ge(s["glu"], ct + 3)
                    pool.wait_ge(s["merged"], ct + 1)
                    win = U[:, bass.ds(ct, 1), :].rearrange("p a c -> p (a c)")[:, SAMPLE0:STREAM]
                    win = bass.AP(win.tensor, win.offset, [win.ap[0], [HIST + DS, DB], [1, DS], [1, W]])
                    taps = K.vec[:, bass.ds(ct, 1), V_DW:V_DW + W].unsqueeze(1).to_broadcast([P, DB, DS, W])
                    nc.gpsimd.tensor_tensor(sprod, win, taps, ALU.mult).then_inc(s["sprod"], 1)
                    for n in range(1, POOLT):
                        pool.wait_ge(s["prod"], POOLT * ct + n + 1)
                        if n > 1:
                            pool.wait_ge(s["added"], (POOLT - 1) * (ct + 1) + n - 1)
                        nc.gpsimd.tensor_tensor(psum_p[u], prods[0] if n == 1 else psum_p[u], prods[n % 3], ALU.add).then_inc(s["added"], 1)
            pool.wait_ge(s["glu"], KT + 2)
            for k in range(KT):
                last = nc.gpsimd.tensor_copy(fresh[:, k, :].rearrange("p (s t) -> p s t", t=DS), samples(k, HIST, DS))
            last.then_inc(s["zero"], 1)

        @block.tensor
        def _(pe):
            pe.wait_ge(s["hist"], 16)
            pe.sem_inc(s["proj"], 2)
            for k in range(KT):
                for a in range(2):
                    last = nc.tensor.transpose(K.ps[k][:, a * NHR:(a + 1) * NHR], hist[0:NHR, a, k * P:(k + 1) * P],
                                               K.ident[0:NHR, 0:NHR])
                last.then_inc(s["histT"], 1)
            pe.wait_ge(s["histout"], KT)
            with pe.Fori(0, loops) as it:
                for u in range(2):
                    pe.wait_ge(s_w[u], 32 * it + 32)
                    pe.wait_ge(s["glu"], 2 * it + u + 1)
                    for h in range(2):
                        for n in range(2):
                            for k in range(KT):
                                last = nc.tensor.matmul(K.ps[4 * u + 2 * h + n][:, 0:HALF], wt[u][:, k, h, :],
                                                        HT[:, k, n * HALF:(n + 1) * HALF], start=(k == 0), stop=(k == KT - 1))
                    last.then_inc(s["proj"], 1)
            pe.wait_ge(s["glu"], KT + 2)
            pe.wait_ge(s["zero"], 2)
            for k in range(KT):
                nc.tensor.transpose(K.ps[k // 4][0:HIST, k % 4 * P:(k % 4 + 1) * P], stream(k, SEQ, SEQ + HIST), K.ident[:])
                last = nc.tensor.transpose(K.ps[2 + k // 4][0:NS, k % 4 * P:(k % 4 + 1) * P], fresh[:, k, :], K.ident[:])
            last.then_inc(s_tr, 1)

        @block.scalar
        def _(act):
            with act.Fori(0, loops) as it:
                for u in range(2):
                    act.wait_ge(s["proj"], 2 * it + u + 3)
                    act.wait_ge(s["glu"], 2 * it + u + 1)
                    K.settle(act)
                    for n in range(2):
                        last = nc.scalar.activation(sg[u][:, n * HALF:(n + 1) * HALF], K.ps[4 * u + 2 + n][:, 0:HALF],
                                                    ACT.Sigmoid, bias=K.vec[:, 2 * it + u, V_B1 + 1:V_B1 + 2])
                    last.then_inc(s["sig"], 1)
                    ct = 2 * it + u
                    act.wait_ge(s["glu"], ct + 3)
                    for n in range(POOLT):
                        act.wait_ge(s["added"], (POOLT - 1) * (ct + 1) + max(n - 3, 1) if n >= 3 else (POOLT - 1) * ct + n + POOLT - 3)
                        K.settle(act)
                        nc.scalar.activation(prods[n % 3], stream(ct, n, n + SEQ), ACT.Copy, scale=K.vec[:, ct, V_DW + n:V_DW + n + 1]).then_inc(s["prod"], 1)
            act.wait_ge(s_tr, 1)
            for q in range(4):
                r = HIST if q < 2 else NS
                nc.scalar.activation(tail[0:r, q // 2, q % 2 * 512:(q % 2 + 1) * 512], K.ps[q][0:r, :], ACT.Copy).then_inc(s_ev, 1)

        @block.vector
        def _(dve):
            dve.sem_inc(s["glu"], 2)
            for k in range(KT):
                dve.wait_ge(s["histT"], k + 1)
                nc.vector.tensor_copy(samples(k, 0, HIST), K.ps[k][:, 0:2 * NHR].rearrange("p (s t) -> p s t", t=HIST)).then_inc(s["histout"], 1)
            dve.wait_ge(s["zero"], 1)
            dve.wait_ge(s["histout"], KT)
            dve.sem_inc(s["merged"], 2)
            taps = W - POOLT + 3
            with dve.Fori(0, loops) as it:
                for u in range(2):
                    ct = 2 * it + u
                    dve.wait_ge(s["sig"], ct + 1)
                    ba = K.vec[:, ct, V_B1:V_B1 + 1]
                    nc.vector.scalar_tensor_tensor(out=stream(ct, HIST, HIST + HALF), in0=K.ps[4 * u][:, 0:HALF], scalar=ba,
                                                   in1=sg[u][:, 0:HALF], op0=ALU.add, op1=ALU.mult)
                    nc.vector.scalar_tensor_tensor(out=stream(ct, HIST + HALF, HIST + SEQ), in0=K.ps[4 * u + 1][:, 0:SEQ - HALF], scalar=ba,
                                                   in1=sg[u][:, HALF:SEQ], op0=ALU.add, op1=ALU.mult)
                    nc.vector.scalar_tensor_tensor(
                        out=samples(ct, HIST, DS), in0=K.ps[4 * u + 1][:, SEQ - HALF:HALF].rearrange("p (s t) -> p s t", t=DS), scalar=ba,
                        in1=sg[u][:, SEQ:TOK].rearrange("p (s t) -> p s t", t=DS), op0=ALU.add, op1=ALU.mult).then_inc(s["gchain"], 1)
                    dve.wait_ge(s["gchain"], ct + 1)
                    dve.sem_inc(s["glu"], 1)
                    bd = K.vec[:, ct, V_BDW:V_BDW + 1]
                    c = C[:, ct, 0:SEQ]
                    for n, j in enumerate(range(POOLT, W)):
                        wj, x = K.vec[:, ct, V_DW + j:V_DW + j + 1], stream(ct, j, j + SEQ)
                        if n >= 2:
                            dve.wait_ge(s["tap"], taps * ct + n - 1)
                        if n == 0:
                            last = nc.vector.tensor_scalar(c, x, wj, bd, ALU.mult, ALU.add)
                        elif n == 1:
                            last = nc.vector.tensor_scalar(C2, x, wj, None, ALU.mult)
                        else:
                            y = C2 if n % 2 else c
                            last = nc.vector.scalar_tensor_tensor(out=y, in0=x, scalar=wj, in1=y, op0=ALU.mult, op1=ALU.add)
                        last.then_inc(s["tap"], 1)
                    n = W - POOLT
                    dve.wait_ge(s["tap"], taps * ct + n)
                    nc.vector.tensor_tensor(c, c, C2, ALU.add).then_inc(s["tap"], 1)
                    dve.wait_ge(s["sprod"], ct + 1)
                    nc.vector.tensor_reduce(sred[u], sprod, AX.X, ALU.add).then_inc(s["sred"], 1)
                    dve.wait_ge(s["sred"], ct + 1)
                    nc.vector.tensor_scalar(C[:, ct, SEQ:TOK], sred[u].rearrange("p s t o -> p (s t o)"), bd, None, ALU.add).then_inc(s["tap"], 1)
                    dve.wait_ge(s["added"], (POOLT - 1) * (ct + 2))
                    dve.wait_ge(s["tap"], taps * ct + n + 1)
                    nc.vector.tensor_tensor(c, c, psum_p[u], ALU.add).then_inc(s["tap"], 1)
                    dve.wait_ge(s["tap"], taps * ct + n + 3)
                    dve.sem_inc(s["merged"], 1)


def stage_conv_out(K):
    nc, d = K.nc, K.d
    names = ("sum", "mean", "centred", "square", "sumsq", "var", "root", "rstd", "scaled", "act", "y", "added", "bias", "b2")
    s = {n: K.sem(f"convout_{n}") for n in names}
    C = K.C
    at = K.conv_end
    sq = K.region(at, KT, TOK); at += KT * TOK
    mean, rstd = K.region(A_HT, TOK), K.region(A_HT + TOK, TOK)
    halves = [slice(0, HALF), slice(HALF, TOK)]

    with nc.Block() as block:
        @block.sync
        def _(sp):
            sp.wait_ge(s["b2"], 16)

        @block.gpsimd
        def _(pool):
            b2 = K.region(A_HN, D)
            pool.dma_start(b2, d["conv_b_pw2"].partition_broadcast(P)).then_inc(s["b2"], 16)
            pool.wait_ge(s["b2"], 16)
            for b, r in enumerate(ROWS):
                last = nc.gpsimd.tensor_tensor(K.X[0:r, b, :], K.X[0:r, b, :], b2[0:r], ALU.add)
            last.then_inc(s["bias"], 1)

        @block.tensor
        def _(pe):
            for h in range(2):
                for k in range(KT):
                    last = nc.tensor.matmul(K.ps[h][:, 0:HALF], K.ones[:], C[:, k, halves[h]], start=(k == 0), stop=(k == KT - 1))
            last.then_inc(s["sum"], 1)
            for k in range(KT):
                pe.wait_ge(s["square"], k + 1)
                for h in range(2):
                    last = nc.tensor.matmul(K.ps[2 + h][:, 0:HALF], K.ones[:], sq[:, k, halves[h]], start=(k == 0), stop=(k == KT - 1))
            last.then_inc(s["sumsq"], 1)
            pe.wait_ge(K.s_w2, 16)
            for b, r in enumerate(ROWS):
                for n in range(2):
                    g = 2 * b + n
                    if g >= 4:
                        pe.wait_ge(s["added"], g - 3)
                    for k in range(KT):
                        if g == 0:
                            pe.wait_ge(s["act"], k + 1)
                        last = nc.tensor.matmul(K.ps[4 + g % 4][0:r, :], C[:, k, b * P:b * P + r], K.w2[:, k, n * 512:(n + 1) * 512],
                                                start=(k == 0), stop=(k == KT - 1))
                    last.then_inc(s["y"], 1)

        @block.scalar
        def _(act):
            for k in range(KT):
                act.wait_ge(s["centred"], k + 1)
                nc.scalar.activation(sq[:, k, :], C[:, k, :], ACT.Square).then_inc(s["square"], 1)
            act.wait_ge(s["var"], 1)
            nc.scalar.activation(rstd, rstd, ACT.Sqrt).then_inc(s["root"], 1)
            for k in range(KT):
                act.wait_ge(s["scaled"], k + 1)
                nc.scalar.activation(C[:, k, :], C[:, k, :], ACT.Silu, bias=K.vec[:, k, V_LNB:V_LNB + 1],
                                     scale=K.vec[:, k, V_LNG:V_LNG + 1]).then_inc(s["act"], 1)

        @block.vector
        def _(dve):
            dve.wait_ge(s["sum"], 1)
            for h in range(2):
                last = nc.vector.tensor_scalar(mean[:, halves[h]], K.ps[h][:, 0:HALF], 1.0 / D, None, ALU.mult)
            last.then_inc(s["mean"], 1)
            dve.wait_ge(s["mean"], 1)
            for k in range(KT):
                nc.vector.tensor_tensor(C[:, k, :], C[:, k, :], mean, ALU.subtract).then_inc(s["centred"], 1)
            dve.wait_ge(s["sumsq"], 1)
            for h in range(2):
                last = nc.vector.tensor_scalar(rstd[:, halves[h]], K.ps[2 + h][:, 0:HALF], 1.0 / D, LN_EPS, ALU.mult, ALU.add)
            last.then_inc(s["var"], 1)
            dve.wait_ge(s["root"], 1)
            nc.vector.reciprocal(rstd, rstd).then_inc(s["rstd"], 1)
            dve.wait_ge(s["rstd"], 1)
            for k in range(KT):
                dve.wait_ge(s["square"], k + 1)
                nc.vector.tensor_tensor(C[:, k, :], C[:, k, :], rstd, ALU.mult).then_inc(s["scaled"], 1)
            dve.wait_ge(s["bias"], 1)
            for b, r in enumerate(ROWS):
                for n in range(2):
                    g = 2 * b + n
                    dve.wait_ge(s["y"], g + 1)
                    x = K.X[0:r, b, n * 512:(n + 1) * 512]
                    nc.vector.tensor_tensor(x, x, K.ps[4 + g % 4][0:r, :], ALU.add).then_inc(s["added"], 1)


def load_expert(K, sp, layer, e, u):
    for m, name in enumerate(("moe_w_gate", "moe_w_up")):
        sp.dma_start(K.region(A_RING + u * EW + m * KT * FE, KT, FE), K.d[name][layer, e].rearrange("(k p) f -> p k f", p=P)).then_inc(K.s_w[u], 16)
    sp.dma_start(K.region(A_RING + u * EW + 2 * KT * FE, FE // P, D), K.d["moe_w_down"][layer, e].rearrange("(j p) c -> p j c", p=P)).then_inc(K.s_w[u], 16)


def stage_route(K, layer):
    nc = K.nc
    K.s_w = [K.sem(f"moe{layer}_w{u}") for u in range(RING)]
    s_part, s_rest = K.sem(f"route{layer}_part"), K.sem(f"route{layer}_rest")
    HN, part = K.HN(), [K.part(i) for i in range(3)]
    names = ("logits", "member", "rank", "exp", "exped", "chain", "pool")
    s = {n: K.sem(f"route{layer}_{n}") for n in names}
    HT = K.HT()
    at = [A_XS]

    def tmp(*dims):
        n = 1
        for x in dims:
            n *= x
        v = K.region(at[0], *dims)
        at[0] += n
        return v

    lg = tmp(NB, NR)
    c8, cm, f8, fm = (tmp(NB, 8) for _ in range(4))
    ci, fi = (tmp(NB, 8).bitcast(U32) for _ in range(2))
    og = tmp(NB, NG)
    prod = tmp(NB, NG, EPG)
    gi, fidx, e1, e2 = (tmp(NB, 1) for _ in range(4))
    ex = tmp(NB, NG + 1)
    esum, gtop, w1 = (tmp(NB, 1) for _ in range(3))
    m1, m2, mm, rk, t1 = (tmp(NB, NE) for _ in range(5))
    cnt, scan, zero, st = (tmp(NE) for _ in range(4))
    mx = tmp(1)
    passes = tmp(NE, NPASS)
    logits = K.ps[0][:, 0:NB * NR].rearrange("p (b r) -> p b r", b=NB)
    ranks = K.ps[1][:, 0:NB * NE].rearrange("p (b r) -> p b r", b=NB)
    counts = K.ps[2][:, 0:NE]

    with nc.Block() as block:
        @block.tensor
        def _(pe):
            for b, r in enumerate(ROWS):
                for k in range(KT):
                    last = nc.tensor.matmul(logits[0:r, b, :], HT[:, k, b * P:b * P + r], K.wr[:, layer, k, :], start=(k == 0), stop=(k == KT - 1))
            last.then_inc(s["logits"], 1)
            pe.wait_ge(s["member"], 1)
            for b in range(NB):
                for b2 in range(b + 1):
                    nc.tensor.matmul(ranks[:, b, :], K.before[:] if b2 == b else K.ones[:], mm[:, b2, :], start=(b2 == 0), stop=(b2 == b))
            for b in range(NB):
                last = nc.tensor.matmul(counts, K.ones[:], mm[:, b, :], start=(b == 0), stop=(b == NB - 1))
            last.then_inc(s["rank"], 1)

        @block.sync
        def _(sp):
            for u in range(2):
                load_expert(K, sp, layer, u, u)

        @block.gpsimd
        def _(pool):
            pool.wait_ge(s["logits"], 1)
            nc.gpsimd.iota(K.region(A_COUNT, SLOTS), pattern=[[1, SLOTS]], base=0, channel_multiplier=0,
                           allow_small_or_imprecise_dtypes=True)
            for i in range(2):
                for b, rr in enumerate(ROWS):
                    pool.wait_ge(s_part, NB * i + b + 1)
                    rest = HN[0:rr, b, :] if i == 0 else part[2][0:rr, b, :]
                    nc.gpsimd.tensor_tensor(rest, HN[0:rr, b, :], part[i][0:rr, b, :], ALU.subtract).then_inc(s_rest, 1)

        @block.scalar
        def _(act):
            for i in range(2):
                for b, rr in enumerate(ROWS):
                    if i == 1:
                        act.wait_ge(s_rest, b + 1)
                    nc.scalar.activation(part[i][0:rr, b, :], HN[0:rr, b, :], ACT.Copy).then_inc(s_part, 1)
            act.wait_ge(s["exp"], 1)
            nc.scalar.activation(ex, ex, ACT.Exp).then_inc(s["exped"], 1)

        @block.vector
        def _(dve):
            do = Chain(dve, s["chain"])
            v = nc.vector
            v.memset(lg, 0.0)
            v.memset(zero, 1.0)
            do(v.memset(c8, NEG))
            dve.wait_ge(s["logits"], 1)
            br = K.br[:, layer, :]
            v.tensor_tensor(lg[:, 0:NB - 1, :], logits[:, 0:NB - 1, :], br.unsqueeze(1).to_broadcast([P, NB - 1, NR]), ALU.add)
            do(v.tensor_tensor(lg[0:NS, NB - 1, :], logits[0:NS, NB - 1, :], br[0:NS], ALU.add))
            do(v.tensor_copy(c8[:, :, 0:NG], lg[:, :, 0:NG]))
            for b in range(NB):
                last = v.max(cm[:, b, :], c8[:, b, :])
            do(last)
            for b in range(NB):
                last = v.max_index(ci[:, b, :], cm[:, b, :], c8[:, b, :])
            do(last)
            do(v.tensor_copy(gi, ci[:, :, 0:1]))
            do(v.tensor_tensor(og, K.iota[:, 0:NG].unsqueeze(1).to_broadcast([P, NB, NG]), gi.to_broadcast([P, NB, NG]), ALU.is_equal))
            for g in range(NG):
                last = v.tensor_tensor(prod[:, :, g, :], lg[:, :, NG + EPG * g:NG + EPG * (g + 1)],
                                       og[:, :, g:g + 1].to_broadcast([P, NB, EPG]), ALU.mult)
            do(last)
            do(v.tensor_reduce(f8, prod.rearrange("p b g e -> p b e g"), AX.X, ALU.add))
            for b in range(NB):
                last = v.max(fm[:, b, :], f8[:, b, :])
            do(last)
            for b in range(NB):
                last = v.max_index(fi[:, b, :], fm[:, b, :], f8[:, b, :])
            do(last)
            for j, e in ((0, e1), (1, e2)):
                do(v.tensor_copy(fidx, fi[:, :, j:j + 1]))
                do(v.scalar_tensor_tensor(out=e, in0=gi, scalar=float(EPG), in1=fidx, op0=ALU.mult, op1=ALU.add))
            for m, e in ((m1, e1), (m2, e2)):
                do(v.tensor_tensor(m, K.iota[:].unsqueeze(1).to_broadcast([P, NB, NE]), e.to_broadcast([P, NB, NE]), ALU.is_equal))
                do(v.tensor_tensor(m, m, K.valid[:].unsqueeze(2).to_broadcast([P, NB, NE]), ALU.mult))
            v.tensor_tensor(mm, m1, m2, ALU.add).then_inc(s["member"], 1)
            v.tensor_tensor(ex[:, :, 0:NG], lg[:, :, 0:NG], cm[:, :, 0:1].to_broadcast([P, NB, NG]), ALU.subtract)
            v.tensor_tensor(ex[:, :, NG:NG + 1], fm[:, :, 1:2], fm[:, :, 0:1], ALU.subtract).then_inc(s["exp"], 1)
            dve.wait_ge(s["exped"], 1)
            do(v.tensor_reduce(esum, ex[:, :, 0:NG], AX.X, ALU.add))
            do(v.reciprocal(gtop, esum))
            do(v.tensor_scalar(w1, ex[:, :, NG:NG + 1], 1.0, None, ALU.add))
            do(v.reciprocal(w1, w1))
            do(v.tensor_tensor(K.wts[:, :, 0:1], gtop, w1, ALU.mult))
            do(v.tensor_tensor(K.wts[:, :, 1:2], K.wts[:, :, 0:1], ex[:, :, NG:NG + 1], ALU.mult))
            dve.wait_ge(s["rank"], 1)
            do(v.tensor_copy(cnt, counts))
            do(v.tensor_tensor_scan(scan, zero, cnt, 0.0, ALU.mult, ALU.add))
            do(v.tensor_tensor(st, scan, cnt, ALU.subtract))
            v.tensor_copy(K.start[:], st)
            for c in range(NPASS):
                last = v.tensor_scalar(passes[:, :, c], st, float(c * CAP), float(SLOTS), ALU.add, ALU.min)
            do(last)
            v.tensor_copy(K.starts[:], passes.rearrange("p e c -> p (e c)"))
            do(v.tensor_reduce(mx, cnt, AX.X, ALU.max))
            do(v.tensor_scalar(mx, mx, float(CAP), None, ALU.is_gt))
            v.tensor_copy(K.over[:], mx)
            do(v.tensor_tensor(rk, ranks, st.unsqueeze(1).to_broadcast([P, NB, NE]), ALU.add))
            for j, m in ((0, m1), (1, m2)):
                do(v.tensor_tensor(t1, rk, m, ALU.mult))
                do(v.tensor_reduce(K.posf[:, :, j:j + 1], t1, AX.X, ALU.add))
            do(v.tensor_copy(K.pos[:], K.posf[:]))


def stage_moe(K, layer):
    nc, d = K.nc, K.d
    L = f"moe{layer}_"
    names = ("pad", "padded", "picked", "turned", "xa", "xv", "chain", "in", "gu", "silu", "h", "y", "ya", "yv", "store")
    s = {n: K.sem(L + n) for n in names}
    XT = K.region(A_XS, KT, XCOLS)
    at = A_HN
    xe = [K.region(at + u * KT * CAP, KT, CAP) for u in range(2)]; at += 2 * KT * CAP
    gs = [K.region(at + u * 2 * CAP, 2 * CAP) for u in range(2)]; at += 4 * CAP
    hT = [K.region(at + u * 2 * CAP, 2, CAP) for u in range(2)]; at += 4 * CAP
    yo = [K.region(at + u * D, D) for u in range(2)]; at += 2 * D
    wg, wu, wd = [], [], []
    for u in range(RING):
        o = A_RING + u * EW
        wg.append(K.region(o, KT, FE))
        wu.append(K.region(o + KT * FE, KT, FE))
        wd.append(K.region(o + 2 * KT * FE, FE // P, D))
    gain = V_FFN + layer
    iters = NE // RING
    NJ = FE // P
    reg = lambda eng, ap, hi: eng.value_load(ap, min_val=0, max_val=hi)

    def gate_up(u, v):
        for m, w in ((0, wg), (1, wu)):
            for j in range(NJ):
                for k in range(KT):
                    last = nc.tensor.matmul(K.ps[2 * v + m][:, j * CAP:(j + 1) * CAP], w[u][:, k, j * P:(j + 1) * P], xe[v][:, k, :],
                                            start=(k == 0), stop=(k == KT - 1))
        return last

    def down(u, v):
        for n in range(2):
            for j in range(NJ):
                last = nc.tensor.matmul(K.ps[4 + 2 * v + n][0:CAP, :], hT[v][:, j, :], wd[u][:, j, n * 512:(n + 1) * 512],
                                        start=(j == 0), stop=(j == NJ - 1))
        return last

    pick = K.region16(A_PICK, NB, SLOTS)
    count = K.region(A_COUNT, SLOTS)
    parts = [K.part(i) for i in range(3)]
    groups = [(i, m) for i in range(len(PIECES)) for m in range(KT)]
    with nc.Block() as block:
        @block.gpsimd
        def _(pool):
            nc.gpsimd.memset(XT[:, :, SLOTS:XCOLS], 0.0).then_inc(s["pad"], 1)

        @block.sync
        def _(sp):
            sp.wait_ge(s["pad"], 1)
            sp.dma_start(K.ys_dram.rearrange("r c -> (r c)")[SLOTS * D:XCOLS * D].rearrange("(p k c) -> p k c", p=P, k=KT), XT[:, :, SLOTS:XCOLS]).then_inc(s["padded"], 16)
            sp.wait_ge(s["padded"], 16)

        @block.tensor
        def _(pe):
            for t, (i, m) in enumerate(groups):
                o, n = PIECES[i]
                if m == 0:
                    pe.wait_ge(s["picked"], NB * (i + 1))
                if t >= 8:
                    pe.wait_ge(s["xv" if t % 2 else "xa"], (t - 8) // 2 + 1)
                for b, rr in enumerate(ROWS):
                    for i, part in enumerate(parts):
                        last = nc.tensor.matmul(K.ps[t % 8][:, 0:n], part[0:rr, b, m * P:(m + 1) * P], pick[0:rr, b, o:o + n],
                                                start=(b == 0 and i == 0), stop=(b == NB - 1 and i == 2))
                last.then_inc(s["turned"], 1)

        def columns_out(eng, mine, scaled):
            for t, (i, m) in enumerate(groups):
                if t % 2 == mine:
                    o, n = PIECES[i]
                    eng.wait_ge(s["turned"], t + 1)
                    scaled(XT[:, m, o:o + n], K.ps[t % 8][:, 0:n], K.vec[:, m, gain:gain + 1]).then_inc(s[("xa", "xv")[mine]], 1)

        @block.scalar
        def _(act):
            columns_out(act, 0, lambda out, i, g: nc.scalar.activation(out, i, ACT.Copy, scale=g))

        @block.vector
        def _(dve):
            do = Chain(dve, s["chain"])
            for o, n in PIECES:
                for b in range(NB):
                    last = nc.vector.tensor_scalar(pick[:, b, o:o + n], count[:, o:o + n], K.posf[:, b, 0:1], None, ALU.is_equal)
                do(last)
                for b in range(NB):
                    nc.vector.scalar_tensor_tensor(out=pick[:, b, o:o + n], in0=count[:, o:o + n], scalar=K.posf[:, b, 1:2],
                                                   in1=pick[:, b, o:o + n], op0=ALU.is_equal, op1=ALU.add).then_inc(s["picked"], 1)
            columns_out(dve, 1, lambda out, i, g: nc.vector.tensor_scalar(out, i, g, None, ALU.mult))

    with nc.Block() as block:
        @block.sync
        def _(sp):
            for u in range(2, RING):
                load_expert(K, sp, layer, u, u)
            with sp.Fori(1, iters) as it:
                for u in range(RING):
                    sp.wait_ge(s["y"], RING * (it - 1) + u + 1)
                    load_expert(K, sp, layer, RING * it + u, u)

        @block.tensor
        def _(pe):
            def one_down(e, u):
                v = u % 2
                pe.wait_ge(s["h"], e + 3)
                pe.wait_ge(s["ya"], e + 1)
                pe.wait_ge(s["yv"], e + 1)
                down(u, v).then_inc(s["y"], 1)

            def body(it):
                for u in range(RING):
                    e, v = RING * it + u, u % 2
                    pe.wait_ge(K.s_w[u], 48 * it + 48)
                    pe.wait_ge(s["in"], e + 1)
                    pe.wait_ge(s["h"], e + 1)
                    gate_up(u, v).then_inc(s["gu"], 1)
                    if not (isinstance(it, int) and e == 0):
                        one_down(e - 1, (u - 1) % RING)

            body(0)
            with pe.Fori(1, iters) as it:
                body(it)
            one_down(NE - 1, RING - 1)

        @block.scalar
        def _(act):
            def half_out(e, v):
                act.wait_ge(s["y"], e + 1)
                if not (isinstance(e, int) and e < 2):
                    act.wait_ge(s["store"], 16 * e - 16)
                nc.scalar.activation(yo[v][0:CAP, 0:512], K.ps[4 + 2 * v][0:CAP, :], ACT.Copy).then_inc(s["ya"], 1)

            def body(it):
                for u in range(RING):
                    e, v = RING * it + u, u % 2
                    act.wait_ge(s["gu"], e + 1)
                    act.wait_ge(s["h"], e + 1)
                    nc.scalar.activation(gs[v], K.ps[2 * v][:, 0:2 * CAP], ACT.Silu).then_inc(s["silu"], 1)
                    if not (isinstance(it, int) and e == 0):
                        half_out(e - 1, 1 - v)

            act.sem_inc(s["ya"], 2)
            body(0)
            with act.Fori(1, iters) as it:
                body(it)
            half_out(NE - 1, 1)

        @block.vector
        def _(dve):
            def product(e, v):
                dve.wait_ge(s["silu"], e + 1)
                if not (isinstance(e, int) and e < 2):
                    dve.wait_ge(s["y"], e - 1)
                nc.vector.tensor_tensor(hT[v], gs[v].rearrange("p (j t) -> p j t", j=NJ),
                                        K.ps[2 * v + 1][:, 0:2 * CAP].rearrange("p (j t) -> p j t", j=NJ), ALU.mult).then_inc(s["h"], 1)

            def half_out(e, v):
                dve.wait_ge(s["y"], e + 1)
                if not (isinstance(e, int) and e < 2):
                    dve.wait_ge(s["store"], 16 * e - 16)
                nc.vector.tensor_copy(yo[v][0:CAP, 512:D], K.ps[5 + 2 * v][0:CAP, :]).then_inc(s["yv"], 1)

            def body(it):
                for u in range(RING):
                    e, v = RING * it + u, u % 2
                    st = reg(dve, K.start[0:1, bass.ds(e, 1)], SLOTS)
                    if not (isinstance(it, int) and e < 2):
                        dve.wait_ge(s["gu"], e - 1)
                    nc.vector.tensor_copy(xe[v], XT[:, :, bass.ds(st, CAP)]).then_inc(s["in"], 1)
                    if not (isinstance(it, int) and e < 1):
                        product(e - 1, 1 - v)
                    if not (isinstance(it, int) and e < 2):
                        half_out(e - 2, v)

            dve.sem_inc(s["h"], 2)
            dve.sem_inc(s["yv"], 2)
            body(0)
            with dve.Fori(1, iters) as it:
                body(it)
            product(NE - 1, 1)
            half_out(NE - 2, 0)
            half_out(NE - 1, 1)

        @block.gpsimd
        def _(pool):
            def body(it):
                for u in range(RING):
                    e, v = RING * it + u, u % 2
                    st = reg(pool, K.start[0:1, bass.ds(e, 1)], SLOTS)
                    pool.wait_ge(s["ya"], e + 3)
                    pool.wait_ge(s["yv"], e + 3)
                    if not (isinstance(it, int) and e == 0):
                        pool.wait_ge(s["store"], 16 * e)
                    pool.dma_start(K.ys_dram[bass.ds(st, CAP), :], yo[v][0:CAP]).then_inc(s["store"], 16)

            body(0)
            with pool.Fori(1, iters) as it:
                body(it)
            pool.wait_ge(s["store"], 16 * NE)

    names = ("in", "gu", "silu", "h", "y", "ya", "yv", "store", "stored")
    r = {n: K.sem(f"{L}all_{n}") for n in names}
    with nc.Block() as block:
        @block.sync
        def _(sp):
            flag = reg(sp, K.over[0:1, 0:1], 1)
            with sp.If(flag > 0):
                with sp.Fori(0, NE) as e:
                    sp.wait_ge(r["y"], NPASS * e + 1)
                    load_expert(K, sp, layer, e, 0)

        @block.tensor
        def _(pe):
            flag = reg(pe, K.over[0:1, 0:1], 1)
            with pe.If(flag > 0):
                pe.sem_inc(r["y"], 1)
                with pe.Fori(0, NE) as e:
                    with pe.Fori(0, NPASS) as c:
                        n = NPASS * e + c
                        pe.wait_ge(K.s_w[0], 48 * iters + 48 * e + 48)
                        pe.wait_ge(r["in"], n + 1)
                        gate_up(0, 0).then_inc(r["gu"], 1)
                        pe.wait_ge(r["h"], n + 1)
                        pe.wait_ge(r["ya"], n + 1)
                        pe.wait_ge(r["yv"], n + 1)
                        down(0, 0).then_inc(r["y"], 1)

        @block.scalar
        def _(act):
            flag = reg(act, K.over[0:1, 0:1], 1)
            with act.If(flag > 0):
                act.sem_inc(r["ya"], 1)
                with act.Fori(0, NE * NPASS) as n:
                    act.wait_ge(r["gu"], n + 1)
                    nc.scalar.activation(gs[0], K.ps[0][:, 0:2 * CAP], ACT.Silu).then_inc(r["silu"], 1)
                    act.wait_ge(r["y"], n + 2)
                    act.wait_ge(r["stored"], n + 1)
                    nc.scalar.activation(yo[0][0:CAP, 0:512], K.ps[4][0:CAP, :], ACT.Copy).then_inc(r["ya"], 1)

        @block.vector
        def _(dve):
            flag = reg(dve, K.over[0:1, 0:1], 1)
            with dve.If(flag > 0):
                dve.sem_inc(r["yv"], 1)
                with dve.Fori(0, NE * NPASS) as n:
                    st = reg(dve, K.starts[0:1, bass.ds(n, 1)], SLOTS)
                    dve.wait_ge(r["y"], n + 1)
                    nc.vector.tensor_copy(xe[0], XT[:, :, bass.ds(st, CAP)]).then_inc(r["in"], 1)
                    dve.wait_ge(r["silu"], n + 1)
                    nc.vector.tensor_tensor(hT[0], gs[0].rearrange("p (j t) -> p j t", j=NJ),
                                            K.ps[1][:, 0:2 * CAP].rearrange("p (j t) -> p j t", j=NJ), ALU.mult).then_inc(r["h"], 1)
                    dve.wait_ge(r["y"], n + 2)
                    dve.wait_ge(r["stored"], n + 1)
                    nc.vector.tensor_copy(yo[0][0:CAP, 512:D], K.ps[5][0:CAP, :]).then_inc(r["yv"], 1)

        @block.gpsimd
        def _(pool):
            flag = reg(pool, K.over[0:1, 0:1], 1)
            with pool.If(flag > 0):
                pool.sem_inc(r["stored"], 1)
                with pool.Fori(0, NE * NPASS) as n:
                    st = reg(pool, K.starts[0:1, bass.ds(n, 1)], SLOTS)
                    pool.wait_ge(r["ya"], n + 2)
                    pool.wait_ge(r["yv"], n + 2)
                    pool.dma_start(K.ys_dram[bass.ds(st, CAP), :], yo[0][0:CAP]).then_inc(r["store"], 16)
                    pool.wait_ge(r["store"], 16 * n + 16)
                    pool.sem_inc(r["stored"], 1)

    s_g = [K.sem(f"{L}rows_back{b}") for b in range(NB)]
    s_c = K.sem(L + "sum")
    Y = K.region(A_HN, NB, 2, D)
    with nc.Block() as block:
        @block.gpsimd
        def _(pool):
            for b, rr in enumerate(ROWS):
                for j in range(2):
                    pool.indirect_dma_start(Y[0:rr, b, j, :], None, K.ys_dram, bass.IndirectOffsetOnAxis(ap=K.pos[0:rr, b, j:j + 1], axis=0)).then_inc(s_g[b], 16)

        @block.vector
        def _(dve):
            do = Chain(dve, s_c)
            for b, rr in enumerate(ROWS):
                dve.wait_ge(s_g[b], 32)
                x = K.X[0:rr, b, :]
                for j in range(2):
                    do(nc.vector.scalar_tensor_tensor(out=x, in0=Y[0:rr, b, j, :], scalar=K.wts[0:rr, b, j:j + 1], in1=x, op0=ALU.mult, op1=ALU.add))


def attention_layout(K):
    at = A_XS
    K.QT, K.KTr = K.region(at, KT, TOK), K.region(at + KT * TOK, KT, TOK)
    K.VN = K.HN()
    at += 2 * KT * TOK
    K.a0 = at
    K.kv_early = at + KT * TOK + NB * D + 4 * KT * P
    K.kv_late = at
    K.s_pages = {n: [K.sem(f"pages_{n}{v}") for v in range(2)] for n in "kv"}
    K.ptab = K.sb("ptab", [1, DB * NPG], I32)
    K.sbb = K.sb("sbb", [P, NH])
    K.s_small = K.sem("attn_small")


def load_pages(K, sp, seq, v, base, name):
    pages = K.region(base, NPG, D)
    npool = K.d["cache_k"].shape[1]
    src = K.d["cache_" + name][0].rearrange("n r h c -> n r (h c)")
    for g in range(NPG):
        page = sp.value_load(K.ptab[0:1, bass.ds(seq * NPG + g, 1)], min_val=0, max_val=npool - 1)
        sp.dma_start(pages[:, g, :], src[page]).then_inc(K.s_pages[name][v], 16)


def stage_qkv(K):
    nc, d = K.nc, K.d
    s = {n: K.sem(f"qkv_{n}") for n in ("proj", "a", "v")}
    s_w = [K.sem(f"qkv_w{u}") for u in range(4)]
    HT = K.HT()
    at = K.a0
    VT = K.region(at, KT, TOK); at += KT * TOK
    KN = K.region(at, NB, D); at += NB * D
    wt = [K.region(at + u * KT * P, KT, P) for u in range(4)]; at += 4 * KT * P
    dst = [K.QT, K.KTr, VT]
    scale = [DH ** -0.5, 1.0, 1.0]
    wsrc = d["sb_w_qkv"][0].rearrange("(k p) (m c) -> m p k c", p=P, c=P)
    U = 4

    with nc.Block() as block:
        @block.sync
        def _(sp):
            sp.dma_start(K.ptab[:], d["page_table"].rearrange("s g -> (s g)").unsqueeze(0)).then_inc(K.s_small, 16)
            sp.dma_start(K.sbb[:], d["sb_logit_bias"].partition_broadcast(P)).then_inc(K.s_small, 16)
            with sp.Fori(0, 3 * KT // U) as it:
                for u in range(U):
                    sp.wait_ge(s["proj"], U * it + u + 1)
                    sp.dma_start(wt[u], wsrc[U * it + u]).then_inc(s_w[u], 16)
            sp.wait_ge(K.s_small, 32)
            load_pages(K, sp, 0, 0, K.kv_early, "k")
            load_pages(K, sp, 0, 0, K.kv_early + NPG * D, "v")

        @block.tensor
        def _(pe):
            pe.sem_inc(s["proj"], U)
            with pe.Fori(0, 3 * KT // U) as it:
                for u in range(U):
                    e = U * it + u
                    pe.wait_ge(s_w[u], 16 * it + 16)
                    pe.wait_ge(s["a"], e + 1)
                    pe.wait_ge(s["v"], e + 1)
                    for n in range(2):
                        for k in range(KT):
                            last = nc.tensor.matmul(K.ps[2 * u + n][:, 0:HALF], wt[u][:, k, :], HT[:, k, n * HALF:(n + 1) * HALF],
                                                    start=(k == 0), stop=(k == KT - 1))
                    last.then_inc(s["proj"], 1)

        @block.scalar
        def _(act):
            act.sem_inc(s["a"], U)
            for part in range(3):
                with act.Fori(0, KT // U) as it:
                    for u in range(U):
                        m = U * it + u
                        act.wait_ge(s["proj"], KT * part + m + U + 1)
                        K.settle(act)
                        nc.scalar.activation(dst[part][:, m, 0:HALF], K.ps[2 * u][:, 0:HALF], ACT.Copy, scale=scale[part]).then_inc(s["a"], 1)

        @block.vector
        def _(dve):
            dve.sem_inc(s["v"], U)
            for part in range(3):
                with dve.Fori(0, KT // U) as it:
                    for u in range(U):
                        m = U * it + u
                        dve.wait_ge(s["proj"], KT * part + m + U + 1)
                        nc.vector.tensor_scalar(dst[part][:, m, HALF:TOK], K.ps[2 * u + 1][:, 0:HALF], scale[part], None, ALU.mult).then_inc(s["v"], 1)

    s = {n: K.sem(f"kvrows_{n}") for n in ("turned", "a", "v", "out")}
    with nc.Block() as block:
        groups = [(src, b, h) for src in range(2) for b in range(NB) for h in range(2)]

        @block.tensor
        def _(pe):
            for t, (src, b, h) in enumerate(groups):
                r = ROWS[b]
                if t >= 8:
                    pe.wait_ge(s["av"[t % 2]], (t - 8) // 2 + 1)
                for q in range(4):
                    last = nc.tensor.transpose(K.ps[t % 8][0:r, q * P:(q + 1) * P], (K.KTr, VT)[src][:, 4 * h + q, b * P:b * P + r], K.ident[:])
                last.then_inc(s["turned"], 1)

        def rows_out(eng, mine, copy):
            for t, (src, b, h) in enumerate(groups):
                if t % 2 == mine:
                    r = ROWS[b]
                    eng.wait_ge(s["turned"], t + 1)
                    copy((KN, K.VN)[src][0:r, b, h * 512:(h + 1) * 512], K.ps[t % 8][0:r, :]).then_inc(s["av"[mine]], 1)

        @block.scalar
        def _(act):
            rows_out(act, 0, lambda o, i: nc.scalar.activation(o, i, ACT.Copy))

        @block.vector
        def _(dve):
            rows_out(dve, 1, nc.vector.tensor_copy)

        @block.sync
        def _(sp):
            for src, (buf, name) in enumerate(((KN, "k_rows"), (K.VN, "v_rows"))):
                sp.wait_ge(s["a"], NB * (src + 1))
                sp.wait_ge(s["v"], NB * (src + 1))
                sp.dma_start(d[name + "_p"][0, 0].rearrange("(b p) h c -> p b (h c)", p=P), buf[:, 0:4, :]).then_inc(s["out"], 16)
                sp.dma_start(d[name + "_s"][0].rearrange("s t h c -> (s t) (h c)"), buf[0:NS, 4, :]).then_inc(s["out"], 16)
            sp.wait_ge(s["out"], 64)


def stage_sample_attention(K):
    nc, d = K.nc, K.d
    names = ("mask", "maskT", "ready", "qb", "ka", "kd", "z", "az", "e", "l", "r", "sp", "spm", "scan", "t", "tt",
             "ea", "atr", "at", "av", "om", "sel", "o", "r2", "c")
    s = {n: K.sem(f"sample_{n}") for n in names}
    OT = K.HT()
    R = NH * DS
    NK = PAST + NS
    base = [K.kv_early, K.kv_late]
    kp = [K.region(b, NPG, D) for b in base]
    vp = [K.region(b + NPG * D, NPG, D) for b in base]
    at = K.kv_late + 2 * NPG * D
    KS = K.region(at, KT, NPG * P); at += KT * NPG * P
    kv_gap = at
    at = K.kv_early + 2 * NPG * D
    spaces = [[kv_gap, K.kv_early], [at, A_END]]

    def rows(*dims, r=P):
        n = 1
        for x in dims:
            n *= x
        space = [x for x in spaces if x[0] + n <= x[1]][0]
        v = K.region(space[0], *dims)[0:r]
        space[0] += n
        return v

    az, spb = (rows(NK, r=R) for _ in range(2))
    A = [rows(NK, r=R) for _ in range(2)]
    AT = [rows((NPG + 1) * R) for _ in range(2)]
    QW = KT * (R + 8)
    qb = [rows(QW) for _ in range(2)]
    neg, m01 = rows(DB, NS, r=R), rows(DB, NS, r=R)
    one_hot = rows(NH, DS, r=R)
    sel, hot_h, bcol = rows(DS, r=R), rows(NH, r=R), rows(1, r=R)
    own = K.sb("own_head", [R, D])
    Om_all = K.sb("own_rows", [P, D])
    Om = Om_all[0:R]
    maskT = Om_all[:, 0:DB * R].rearrange("p (s c) -> p s c", s=DB)
    ones_row = K.ones[0:R, 0:1].to_broadcast([R, NK])
    z = K.psum[0:R, 1024:1024 + NK]
    znew = K.psum[0:R, 1024 + PAST:1024 + NK]
    TB = (0, 1, 4)
    O = K.psum[0:R, 5 * 512:7 * 512]
    picked = K.ps[3][:, 64:64 + KT * DS]
    mm = nc.tensor.matmul

    def static_below(x, n):
        return isinstance(x, int) and x < n

    with nc.Block() as block:
        @block.sync
        def _(sp):
            def body(it, us):
                for u in us:
                    seq = 2 * it + u
                    if not static_below(seq, 2):
                        sp.wait_ge(s["t"], KT * (seq - 1))
                        K.settle(sp)
                    load_pages(K, sp, seq, u, base[u], "k")
                    if not static_below(seq, 2):
                        sp.wait_ge(s["av"], seq - 1)
                        K.settle(sp)
                    load_pages(K, sp, seq, u, base[u] + NPG * D, "v")
            body(0, (1,))
            with sp.Fori(1, DB // 2) as it:
                body(it, (0, 1))

        @block.gpsimd
        def _(pool):
            g = nc.gpsimd
            v4 = maskT.rearrange("p s (h t) -> p s h t", t=DS)
            g.memset(maskT, 1.0)
            g.memset(one_hot, 0.0)
            g.memset(own[:], 1.0).then_inc(s["mask"], 1)
            pool.wait_ge(s["mask"], 1)
            g.affine_select(out=v4, in_=v4, compare_op=ALU.is_ge, fill=0.0, base=0,
                            pattern=[[-DS, DB], [0, NH], [0, DS]], channel_multiplier=1)
            o3 = own[:].rearrange("r (h c) -> r h c", h=NH)
            g.affine_select(out=o3, in_=o3, compare_op=ALU.is_ge, fill=0.0, base=0,
                            pattern=[[-DS, NH], [0, DH]], channel_multiplier=1).then_inc(s["mask"], 1)
            pool.wait_ge(s["mask"], 2)
            g.affine_select(out=v4, in_=v4, compare_op=ALU.is_gt, fill=0.0, base=0,
                            pattern=[[DS, DB], [0, NH], [1, DS]], channel_multiplier=-1)
            g.affine_select(out=o3, in_=o3, compare_op=ALU.is_ge, fill=0.0, base=DS - 1,
                            pattern=[[DS, NH], [0, DH]], channel_multiplier=-1)
            g.affine_select(out=one_hot, in_=one_hot, compare_op=ALU.not_equal, fill=1.0, base=0,
                            pattern=[[-DS, NH], [-1, DS]], channel_multiplier=1).then_inc(s["mask"], 1)

        @block.tensor
        def _(pe):
            def weights_turned(e, w):
                pe.wait_ge(s["ea"], e + 1)
                if not static_below(e, 1):
                    pe.wait_ge(s["at"], e)
                K.settle(pe)
                for g in range(NPG):
                    nc.tensor.transpose(K.ps[7][:, g * R:(g + 1) * R], A[w][:, g * P:(g + 1) * P], K.ident[0:R, 0:R])
                nc.tensor.transpose(K.ps[7][0:NS, NPG * R:(NPG + 1) * R], A[w][:, PAST:NK], K.ident[0:R, 0:R]).then_inc(s["atr"], 1)

            def pick(e):
                pe.wait_ge(s["om"], e + 1)
                for m in range(KT):
                    last = mm(picked[:, DS * m:DS * (m + 1)], Om[:, m * P:(m + 1) * P], sel, start=True, stop=True)
                last.then_inc(s["sel"], 1)

            def values(e, w, it):
                pe.wait_ge(s["at"], e + 1)
                pe.wait_ge(K.s_pages["v"][w], NPG * 16 * (it + 1))
                if not static_below(e, 1):
                    pe.wait_ge(s["om"], e)
                for n in range(2):
                    cols = slice(n * 512, (n + 1) * 512)
                    for g in range(NPG):
                        mm(O[:, cols], AT[w][:, g * R:(g + 1) * R], vp[w][:, g, cols], start=(g == 0), stop=False)
                    last = mm(O[:, cols], AT[w][0:NS, NPG * R:(NPG + 1) * R], K.VN[0:NS, NB - 1, cols], start=False, stop=True)
                last.then_inc(s["av"], 1)

            def body(it):
                for v in range(2):
                    e = 2 * it + v
                    pe.wait_ge(K.s_pages["k"][v], NPG * 16 * (it + 1))
                    for m in range(KT):
                        m2, e2 = (m - 3, e) if m >= 3 else (m + 5, e - 1)
                        if not static_below(e2, 0):
                            pe.wait_ge(s["kd" if m2 % 2 else "ka"], 4 * e2 + m2 // 2 + 1)
                        for g in range(NPG):
                            last = nc.tensor.transpose(K.ps[TB[m % 3]][:, g * P:(g + 1) * P], kp[v][:, g, m * P:(m + 1) * P], K.ident[:])
                        last.then_inc(s["t"], 1)
                    if not static_below(e, 1):
                        weights_turned(e - 1, 1 - v)
                    if not static_below(e, 2):
                        pick(e - 2)
                    pe.wait_ge(s["qb"], e + 1)
                    pe.wait_ge(s["ka"], 4 * e + 4)
                    pe.wait_ge(s["kd"], 4 * e + 4)
                    if not static_below(e, 1):
                        pe.wait_ge(s["tt"], e)
                    for m in range(KT):
                        mm(z[:, 0:PAST], qb[v][:, m * R:(m + 1) * R], KS[:, m, :], start=(m == 0), stop=(m == KT - 1))
                    if not static_below(e, 2):
                        pe.wait_ge(s["o"], e - 1)
                    for m in range(KT):
                        last = mm(znew, qb[v][:, m * R:(m + 1) * R], K.KTr[:, m, SEQ:TOK], start=(m == 0), stop=(m == KT - 1))
                    last.then_inc(s["z"], 1)
                    if not static_below(e, 1):
                        values(e - 1, 1 - v, it if v else it - 1)

            pe.wait_ge(s["mask"], 3)
            for q in range(DB):
                last = nc.tensor.transpose(K.ps[7][0:R, q * NS:(q + 1) * NS], maskT[0:NS, q, :], K.ident[0:NS, 0:NS])
            last.then_inc(s["maskT"], 1)
            pe.wait_ge(s["ready"], 1)
            body(0)
            with pe.Fori(1, DB // 2) as it:
                body(it)
            weights_turned(DB - 1, 1)
            pick(DB - 2)
            values(DB - 1, 1, DB // 2 - 1)
            pe.wait_ge(s["o"], DB - 1)
            pick(DB - 1)

        def keys_out(eng, e, mine, copy):
            if not static_below(e, 1):
                eng.wait_ge(s["z"], e)
            for m in range(mine, KT, 2):
                eng.wait_ge(s["t"], KT * e + m + 1)
                copy(KS[:, m, :], K.ps[TB[m % 3]][:]).then_inc(s["kd" if mine else "ka"], 1)

        @block.scalar
        def _(act):
            def turned_out(e, w):
                act.wait_ge(s["atr"], e + 1)
                if not static_below(e, 2):
                    act.wait_ge(s["av"], e - 1)
                nc.scalar.activation(AT[w][:, 0:NPG * R], K.ps[7][:, 0:NPG * R], ACT.Copy)
                nc.scalar.activation(AT[w][0:NS, NPG * R:(NPG + 1) * R], K.ps[7][0:NS, NPG * R:(NPG + 1) * R], ACT.Copy).then_inc(s["at"], 1)

            def body(it):
                for v in range(2):
                    e = 2 * it + v
                    keys_out(act, e, 0, lambda a, b: nc.scalar.activation(a, b, ACT.Copy))
                    if not static_below(e, 1):
                        turned_out(e - 1, 1 - v)
                        act.wait_ge(s["sp"], e)
                    act.wait_ge(s["z"], e + 1)
                    nc.scalar.activation(az, z, ACT.Abs, bias=bcol).then_inc(s["az"], 1)
                    act.wait_ge(s["az"], e + 1)
                    nc.scalar.activation(az, az, ACT.Exp, scale=-1.0).then_inc(s["e"], 1)
                    act.wait_ge(s["e"], e + 1)
                    nc.scalar.activation(az, az, ACT.Ln, bias=1.0).then_inc(s["l"], 1)
                    act.wait_ge(s["tt"], e + 1)
                    nc.scalar.activation(A[v], A[v], ACT.Exp).then_inc(s["ea"], 1)

            body(0)
            with act.Fori(1, DB // 2) as it:
                body(it)
            turned_out(DB - 1, 1)

        @block.vector
        def _(dve):
            vec = nc.vector

            def own_features(e):
                dve.wait_ge(s["av"], e + 1)
                vec.tensor_tensor(Om, O, own[:], ALU.mult).then_inc(s["om"], 1)

            def heads_out(e):
                dve.wait_ge(s["sel"], e + 1)
                vec.tensor_copy(OT[:, :, bass.ds(SEQ + DS * e, DS)], picked.rearrange("p (m t) -> p m t", m=KT)).then_inc(s["o"], 1)

            def body(it):
                for v in range(2):
                    e = 2 * it + v
                    if not static_below(e, 2):
                        dve.wait_ge(s["z"], e - 1)
                    diag = qb[v].rearrange("p (m c) -> p m c", c=R + 8)
                    for q in range(2):
                        last = vec.tensor_copy(diag[64 * q:64 * q + 64, :, DS * q:DS * q + DS], K.QT[64 * q:64 * q + 64, :, bass.ds(SEQ + DS * e, DS)])
                    last.then_inc(s["qb"], 1)
                    keys_out(dve, e, 1, vec.tensor_copy)
                    if not static_below(e, 2):
                        heads_out(e - 2)
                    dve.wait_ge(s["az"], e + 1)
                    vec.tensor_scalar(spb, z, bcol, 0.0, ALU.add, ALU.max).then_inc(s["r"], 1)
                    dve.wait_ge(s["r"], e + 1)
                    dve.wait_ge(s["l"], e + 1)
                    vec.tensor_tensor(spb, spb, az, ALU.add).then_inc(s["sp"], 1)
                    dve.wait_ge(s["sp"], e + 1)
                    new = spb[:, PAST:NK]
                    vec.tensor_tensor(new, new, m01[:, bass.ds(e, 1), :].rearrange("p a c -> p (a c)"), ALU.mult).then_inc(s["spm"], 1)
                    dve.wait_ge(s["spm"], e + 1)
                    vec.tensor_tensor_scan(spb[:, ::-1], ones_row, spb[:, ::-1], 0.0, ALU.mult, ALU.add).then_inc(s["scan"], 1)
                    dve.wait_ge(s["scan"], e + 1)
                    if not static_below(e, 2):
                        dve.wait_ge(s["atr"], e - 1)
                    vec.scalar_tensor_tensor(out=A[v], in0=z, scalar=bcol, in1=spb, op0=ALU.add, op1=ALU.subtract).then_inc(s["r2"], 1)
                    dve.wait_ge(s["r2"], e + 1)
                    new = A[v][:, PAST:NK]
                    vec.tensor_tensor(new, new, neg[:, bass.ds(e, 1), :].rearrange("p a c -> p (a c)"), ALU.add).then_inc(s["tt"], 1)
                    if not static_below(e, 1):
                        own_features(e - 1)

            do = Chain(dve, s["c"])
            vec.memset(qb[0], 0.0)
            vec.memset(qb[1], 0.0)
            dve.wait_ge(s["mask"], 3)
            do(vec.tensor_reduce(sel.unsqueeze(2), one_hot.rearrange("p h t -> p t h"), AX.X, ALU.add))
            do(vec.tensor_reduce(hot_h.unsqueeze(2), one_hot, AX.X, ALU.add))
            do(vec.tensor_tensor(hot_h, hot_h, K.sbb[0:R, :], ALU.mult))
            do(vec.tensor_reduce(bcol, hot_h, AX.X, ALU.add))
            dve.wait_ge(s["maskT"], 1)
            do(vec.tensor_copy(m01.rearrange("p s k -> p (s k)"), K.ps[7][0:R, 0:DB * NS]))
            do(vec.tensor_scalar(neg, m01, -1.0, -NEG, ALU.add, ALU.mult))
            dve.sem_inc(s["ready"], 1)
            body(0)
            with dve.Fori(1, DB // 2) as it:
                body(it)
            heads_out(DB - 2)
            own_features(DB - 1)
            heads_out(DB - 1)


def stage_prompt_attention(K):
    nc, d = K.nc, K.d
    names = ("qk", "v", "z", "az", "r", "e", "l", "sp", "spm", "cum", "ea", "am", "av", "o")
    s = {n: K.sem(f"prompt_{n}") for n in names}
    OT = K.HT()
    nkb = SEQ // P
    off, width = [0, 512, 1024, 896], [SEQ - P * kb for kb in range(4)]
    NC = sum(width)
    at = K.a0
    az = [K.region(at + v * NC, NC) for v in range(2)]; at += 2 * NC
    sp_ = [K.region(at + v * NC, NC) for v in range(2)]; at += 2 * NC
    A = [K.region(at + v * NC, NC) for v in range(2)]; at += 2 * NC
    qs = [K.region(at + v * SEQ, SEQ) for v in range(2)]; at += 2 * SEQ
    ks = [K.region(at + v * SEQ, SEQ) for v in range(2)]; at += 2 * SEQ
    vs = [K.region(at + v * SEQ, nkb, P) for v in range(2)]; at += 2 * SEQ
    assert at <= K.kv_early
    K.wo = K.region(K.kv_early, KT, D)
    K.s_wo = K.sem("wo")
    z = [K.psum[:, 1536 * v:1536 * v + NC] for v in range(2)]
    mm = nc.tensor.matmul
    iters = KT // 2

    def static_below(x, n):
        return isinstance(x, int) and x < n

    with nc.Block() as block:
        @block.sync
        def _(sp):
            sp.dma_start(K.wo, d["sb_w_o"][0].rearrange("(k p) c -> p k c", p=P)).then_inc(K.s_wo, 16)

        def heads(body):
            def four(it):
                for w in range(4):
                    body(2 * it + w // 2, w // 2, 4 * it + w, w % 2)
            return four

        def run(eng, body):
            four = heads(body)
            four(0)
            with eng.Fori(1, iters) as it:
                four(it)

        @block.tensor
        def _(pe):
            def sums(e, v):
                pe.wait_ge(s["spm"], e + 1)
                for kb in range(nkb):
                    last = mm(z[v][:, off[kb]:off[kb] + width[kb]], K.negtri[:], sp_[v][:, off[kb]:off[kb] + width[kb]], start=False, stop=(kb == nkb - 1), skip_group_check=True)
                    for k2 in range(kb + 1, nkb):
                        lo = off[kb] + P * (k2 - kb)
                        mm(z[v][:, lo:lo + width[k2]], K.negones[:], sp_[v][:, off[k2]:off[k2] + width[k2]], start=False, stop=False, skip_group_check=True)
                return last

            def values(m, pv, e, v):
                pe.wait_ge(s["am"], e + 1)
                if v == 0:
                    pe.wait_ge(s["v"], m + 1)
                    if not static_below(m, 2):
                        pe.wait_ge(s["o"], m - 1)
                out = K.ps[6 + pv][64 * v:64 * v + 64, :]
                for kb in range(nkb):
                    last = mm(out[:, P * kb:SEQ], vs[pv][:, kb, 64 * v:64 * v + 64], A[v][:, off[kb]:off[kb] + width[kb]],
                              start=(kb == 0), stop=(kb == nkb - 1), skip_group_check=True)
                last.then_inc(s["av"], 1)

            def body(m, pv, e, v):
                if v == 0:
                    pe.wait_ge(s["qk"], m + 1)
                if not static_below(e, 2):
                    pe.wait_ge(s["ea"], e - 1)
                half = slice(64 * v, 64 * v + 64)
                for kb in (0, 1, 3, 2):
                    last = mm(z[v][:, off[kb]:off[kb] + width[kb]], ks[pv][half, P * kb:P * kb + P], qs[pv][half, P * kb:SEQ],
                              start=(kb != 3), stop=(kb == 2), skip_group_check=True)
                last.then_inc(s["z"], 1)
                if not static_below(e, 1):
                    sums(e - 1, 1 - v).then_inc(s["cum"], 1)
                if not static_below(e, 2):
                    values(m - 1, 1 - pv, e - 2, v)

            run(pe, body)
            sums(NH - 1, 1).then_inc(s["cum"], 1)
            values(KT - 1, 1, NH - 2, 0)
            values(KT - 1, 1, NH - 1, 1)

        @block.scalar
        def _(act):
            def weights(e, v):
                act.wait_ge(s["cum"], e + 1)
                if not static_below(e, 2):
                    act.wait_ge(s["av"], e - 1)
                K.settle(act)
                nc.scalar.activation(A[v], z[v], ACT.Exp, bias=K.sbb[:, bass.ds(e, 1)]).then_inc(s["ea"], 1)

            def body(m, pv, e, v):
                act.wait_ge(s["z"], e + 1)
                if not static_below(e, 2):
                    act.wait_ge(s["sp"], e - 1)
                K.settle(act)
                nc.scalar.activation(az[v], z[v], ACT.Abs, bias=K.sbb[:, bass.ds(e, 1)]).then_inc(s["az"], 1)
                act.wait_ge(s["az"], e + 1)
                nc.scalar.activation(az[v], az[v], ACT.Exp, scale=-1.0).then_inc(s["e"], 1)
                act.wait_ge(s["e"], e + 1)
                nc.scalar.activation(az[v], az[v], ACT.Ln, bias=1.0).then_inc(s["l"], 1)
                if not static_below(e, 1):
                    weights(e - 1, 1 - v)

            run(act, body)
            weights(NH - 1, 1)

        @block.vector
        def _(dve):
            def pair_out(m, pv):
                dve.wait_ge(s["av"], 2 * m + 2)
                nc.vector.tensor_copy(OT[:, bass.ds(m, 1), 0:SEQ].rearrange("p a c -> p (a c)"), K.ps[6 + pv][:]).then_inc(s["o"], 1)

            def body(m, pv, e, v):
                dve.wait_ge(s["az"], e + 1)
                if not static_below(e, 2):
                    dve.wait_ge(s["cum"], e - 1)
                nc.vector.tensor_scalar(sp_[v], z[v], K.sbb[:, bass.ds(e, 1)], 0.0, ALU.add, ALU.max).then_inc(s["r"], 1)
                dve.wait_ge(s["r"], e + 1)
                dve.wait_ge(s["l"], e + 1)
                nc.vector.tensor_tensor(sp_[v], sp_[v], az[v], ALU.add).then_inc(s["sp"], 1)
                if v == 1 and not static_below(m, 1):
                    pair_out(m - 1, 1 - pv)

            run(dve, body)
            pair_out(KT - 1, 1)

        @block.gpsimd
        def _(pool):
            def diagonals(t):
                K.settle(pool)
                for kb in range(nkb):
                    x = t[:, off[kb]:off[kb] + P]
                    last = nc.gpsimd.affine_select(out=x, in_=x, compare_op=ALU.is_gt, fill=0.0, base=0, pattern=[[1, P]], channel_multiplier=-1)
                return last

            def stage_qk(m, pv):
                nc.gpsimd.tensor_copy(qs[pv], K.QT[:, bass.ds(m, 1), 0:SEQ].rearrange("p a c -> p (a c)"))
                nc.gpsimd.tensor_copy(ks[pv], K.KTr[:, bass.ds(m, 1), 0:SEQ].rearrange("p a c -> p (a c)")).then_inc(s["qk"], 1)

            def stage_v(m, pv):
                nc.gpsimd.tensor_copy(vs[pv], K.VN[:, 0:nkb, bass.ds(m * P, P)]).then_inc(s["v"], 1)

            def masked_weights(e, v):
                pool.wait_ge(s["ea"], e + 1)
                diagonals(A[v]).then_inc(s["am"], 1)

            def body(m, pv, e, v):
                if v == 0:
                    if not static_below(m, 1):
                        stage_v(m, pv)
                pool.wait_ge(s["sp"], e + 1)
                diagonals(sp_[v]).then_inc(s["spm"], 1)
                if not static_below(e, 1):
                    masked_weights(e - 1, 1 - v)
                if v == 1:
                    if not (isinstance(m, int) and m == KT - 1):
                        stage_qk(m + 1, 1 - pv)
                    if not static_below(m, 1):
                        pool.wait_ge(s["av"], 2 * m)

            stage_qk(0, 0)
            stage_v(0, 0)
            four = heads(body)
            four(0)
            with pool.Fori(1, iters - 1) as it:
                four(it)
            four(iters - 1)
            masked_weights(NH - 1, 1)


def stage_project(K, tag, src, w, s_w):
    nc = K.nc
    s = {n: K.sem(f"{tag}_{n}") for n in ("y", "added")}
    with nc.Block() as block:
        @block.tensor
        def _(pe):
            pe.wait_ge(s_w, 16)
            for b, r in enumerate(ROWS):
                for n in range(2):
                    g = 2 * b + n
                    if g >= 8:
                        pe.wait_ge(s["added"], g - 7)
                    for k in range(KT):
                        last = nc.tensor.matmul(K.ps[g % 8][0:r, :], src[:, k, b * P:b * P + r], w[:, k, n * 512:(n + 1) * 512],
                                                start=(k == 0), stop=(k == KT - 1))
                    last.then_inc(s["y"], 1)

        @block.vector
        def _(dve):
            for b, r in enumerate(ROWS):
                for n in range(2):
                    g = 2 * b + n
                    dve.wait_ge(s["y"], g + 1)
                    x = K.X[0:r, b, n * 512:(n + 1) * 512]
                    nc.vector.tensor_tensor(x, x, K.ps[g % 8][0:r, :], ALU.add).then_inc(s["added"], 1)


def stage_final(K):
    nc, d = K.nc, K.d
    s = {n: K.sem(f"final_{n}") for n in ("g", "sq", "ms", "root", "rstd", "y", "out")}
    Y, g = K.HN(), K.region(A_HT, D)
    with nc.Block() as block:
        @block.sync
        def _(sp):
            sp.dma_start(g, d["norm_final"].partition_broadcast(P)).then_inc(s["g"], 16)
            for b, r in enumerate(ROWS):
                sp.wait_ge(s["y"], b + 1)
                dst = d["y_prompt"][0, b * P:(b + 1) * P, :] if b < NB - 1 else d["y_sample"].rearrange("s t c -> (s t) c")
                sp.dma_start(dst, Y[0:r, b, :]).then_inc(s["out"], 16)
            sp.wait_ge(s["out"], 16 * NB)

        @block.scalar
        def _(act):
            for b, r in enumerate(ROWS):
                nc.scalar.activation(Y[0:r, b, :], K.X[0:r, b, :], ACT.Square, accum_out=K.ss[0:r, b:b + 1]).then_inc(s["sq"], 1)
            act.wait_ge(s["ms"], 1)
            nc.scalar.activation(K.rstd[:], K.ss[:], ACT.Sqrt).then_inc(s["root"], 1)

        @block.vector
        def _(dve):
            dve.wait_ge(s["sq"], NB)
            nc.vector.tensor_scalar(K.ss[:], K.ss[:], 1.0 / D, NORM_EPS, ALU.mult, ALU.add).then_inc(s["ms"], 1)
            dve.wait_ge(s["root"], 1)
            nc.vector.reciprocal(K.rstd[:], K.rstd[:]).then_inc(s["rstd"], 1)
            dve.wait_ge(s["rstd"], 1)
            dve.wait_ge(s["g"], 16)
            for b, r in enumerate(ROWS):
                nc.vector.scalar_tensor_tensor(out=Y[0:r, b, :], in0=K.X[0:r, b, :], scalar=K.rstd[0:r, b:b + 1], in1=g[0:r],
                                               op0=ALU.mult, op1=ALU.mult).then_inc(s["y"], 1)


def build(nc, dram, stages):
    with ExitStack() as ctx:
        K = Kernel(nc, ctx, dram)
        for st in stages(K):
            st()


def program(K):
    return [
        lambda: stage_setup(K),
        lambda: stage_norm(K, "mix0", V_MIX),
        lambda: stage_conv_in(K),
        lambda: stage_conv_out(K),
        lambda: stage_norm(K, "ffn0", V_FFN),
        lambda: stage_route(K, 0),
        lambda: stage_moe(K, 0),
        K.recycle,
        lambda: attention_layout(K),
        lambda: stage_norm(K, "mix1", V_MIX + 1),
        lambda: stage_qkv(K),
        lambda: stage_sample_attention(K),
        lambda: stage_prompt_attention(K),
        lambda: stage_project(K, "wo", K.HT(), K.wo, K.s_wo),
        lambda: stage_norm(K, "ffn1", V_FFN + 1),
        lambda: stage_route(K, 1),
        lambda: stage_moe(K, 1),
        lambda: stage_final(K),
    ]


INPUTS = ["x_prompt", "x_sample", "state_conv", "cache_k", "cache_v", "page_table", "norm_mix", "norm_ffn", "norm_final",
          "conv_w_pw1", "conv_b_pw1", "conv_w_dw", "conv_b_dw", "conv_ln_g", "conv_ln_b", "conv_w_pw2", "conv_b_pw2",
          "sb_w_qkv", "sb_w_o", "sb_logit_bias", "moe_w_coarse", "moe_b_coarse", "moe_w_fine", "moe_b_fine",
          "moe_w_gate", "moe_w_up", "moe_w_down"]
OUTPUTS = {
    "y_prompt": (1, SEQ, D), "y_sample": (DB, DS, D), "conv_state_p": (1, 1, HIST, D), "conv_state_s": (1, DB, HIST, D),
    "k_rows_p": (1, 1, SEQ, NH, DH), "v_rows_p": (1, 1, SEQ, NH, DH),
    "k_rows_s": (1, DB, DS, NH, DH), "v_rows_s": (1, DB, DS, NH, DH),
}


def kernel(**inputs):
    import numpy as np
    import concourse.bacc as bacc
    from concourse.bass_utils import run_bass_kernel_spmd

    nc = bacc.Bacc("TRN2", target_bir_lowering=False, num_devices=1)
    dram, arrays = {}, {}
    for name in INPUTS:
        a = np.ascontiguousarray(inputs[name])
        arrays[name] = a
        dram[name] = nc.dram_tensor(name, a.shape, mybir.dt.from_np(a.dtype), kind="ExternalInput").ap()
    for name, shape in OUTPUTS.items():
        dram[name] = nc.dram_tensor(name, shape, F32, kind="ExternalOutput").ap()
    build(nc, dram, program)
    r = run_bass_kernel_spmd(nc, [arrays], core_ids=[0])
    return tuple(r.results[0][name] for name in OUTPUTS)
```

```python
import concourse.bass as bass
from concourse import mybir
import numpy as np
from contextlib import ExitStack

F32 = mybir.dt.float32
BF16 = mybir.dt.bfloat16
I32 = mybir.dt.int32
U32 = mybir.dt.uint32
ALU = mybir.AluOpType
ACT = mybir.ActivationFunctionType
AX = mybir.AxisListType

P = 128
D = 1024
KT = D // P
SEQ = 512
DB, DS = 8, 4
NS = DB * DS
TOK = SEQ + NS
NB = SEQ // P + 1
ROWS = [P] * (SEQ // P) + [NS]
HALF = TOK // 2
W = 31
POOLT = 12
HIST = W - 1
STREAM = HIST + SEQ + DB * (HIST + DS)
SAMPLE0 = HIST + SEQ
NH, DH = 16, 64
PAST, PAGE = 512, 128
NPG = PAST // PAGE
NG, EPG = 4, 8
NE = NG * EPG
NR = NG + NE
FE = D // 4
SLOTS = 2 * TOK
CAP = 64
NPASS = 2 * -(-TOK // (2 * CAP))
XCOLS = SLOTS + CAP
RING = 4
NORM_EPS, LN_EPS = 1e-6, 1e-5
NEG = -1.0e30
V_DW, V_MIX, V_FFN, V_B1, V_BDW, V_LNG, V_LNB, NV = 0, 31, 33, 35, 37, 38, 39, 40
A_HN = 0
A_HT = A_HN + NB * D
A_XS = A_HT + KT * TOK + 32
A_RING = A_XS + KT * XCOLS + 256
EW = 3 * KT * FE
A_END = A_RING + RING * EW
PIECE = 364
PIECES = [(o, min(PIECE, SLOTS - o)) for o in range(0, SLOTS, PIECE)]
A_PARTS = [A_HT, A_HN, A_HN + NB * D // 2]
A_PICK = A_HT + NB * D // 2
assert A_PICK + NB * PIECE <= A_XS


class Chain:

    def __init__(self, eng, sem):
        self.eng, self.sem, self.n = eng, sem, 0

    def __call__(self, ins):
        self.n += 1
        ins.then_inc(self.sem, 1)
        self.eng.wait_ge(self.sem, self.n)


class LoopChain:

    def __init__(self, eng, sem, it, per):
        self.eng, self.sem, self.it, self.per, self.n = eng, sem, it, per, 0

    def __call__(self, ins):
        self.n += 1
        assert self.n <= self.per
        ins.then_inc(self.sem, 1)
        self.eng.wait_ge(self.sem, self.it * self.per + self.n)


class Kernel:

    def __init__(self, nc, ctx, dram):
        self.nc, self.ctx, self.d = nc, ctx, dram
        self.sems = []
        self.settled = nc.alloc_semaphore(name="waits_carried")
        self.X = self.sb("X", [P, NB, D])
        self.arena = self.sb("arena", [P, A_END])
        self.ident = self.sb("ident", [P, P])
        self.before = self.sb("before", [P, P])
        self.negtri = self.sb("negtri", [P, P])
        self.ones = self.sb("ones", [P, P])
        self.negones = self.sb("negones", [P, P])
        self.count = self.sb("count", [P, PIECE])
        self.iota = self.count[:, 0:NE]
        self.valid = self.sb("valid", [P, NB])
        self.vec = self.sb("vec", [P, KT, NV])
        self.wr = self.sb("wr", [P, 2, KT, NR])
        self.br = self.sb("br", [P, 2, NR])
        self.ss = self.sb("ss", [P, NB])
        self.rstd = self.sb("rstd", [P, NB])
        self.wts = self.sb("wts", [P, NB, 2])
        self.pos = self.sb("pos", [P, NB, 2], I32)
        self.posf = self.sb("posf", [P, len(PIECES), NB, 2])
        self.start = self.sb("start", [P, NE + 2], I32)
        self.early = self.sb("early", [P, RING], I32)
        self.starts = self.sb("starts", [P, NE * NPASS], I32)
        self.over = self.sb("over", [P, 1], I32)
        self.psum = ctx.enter_context(nc.psum_tensor("psum", [P, 8 * 512], F32))
        self.ps = [self.psum[:, 512 * i:512 * i + 512] for i in range(8)]
        self.ys_dram = nc.dram_tensor("slots_out", [XCOLS, D], F32, kind="Internal").ap()

    def sb(self, name, shape, dt=F32):
        return self.ctx.enter_context(self.nc.sbuf_tensor(name, shape, dt))

    def sem(self, name):
        self.sems.append(self.nc.alloc_semaphore(name=name))
        return self.sems[-1]

    def settle(self, eng):
        eng.sem_inc(self.settled, 1)

    def recycle(self):
        self.nc.clear_and_free_semaphores(self.sems)
        self.nc.all_engine_barrier()
        self.sems = []

    def region(self, at, *dims):
        n = 1
        for x in dims:
            n *= x
        assert at + n <= A_END
        v = self.arena[:, at:at + n]
        if len(dims) == 1:
            return v
        names = "abcd"[:len(dims)]
        return v.rearrange(f"p ({' '.join(names)}) -> p {' '.join(names)}", **dict(zip(names[1:], dims[1:])))

    def HN(self):
        return self.region(A_HN, NB, D)

    def region16(self, at, *dims):
        n = int(np.prod(dims))
        v = self.arena[:, at:at + n // 2].bitcast(BF16)
        return v.rearrange("p (a b) -> p a b", b=dims[1])

    def part(self, i):
        return self.region16(A_PARTS[i], NB, D)

    def HT(self):
        return self.region(A_HT, KT, TOK)


def square_sums(K, act, sem, per_block, scratch):
    for b, r in enumerate(ROWS):
        if per_block:
            act.wait_ge(sem, per_block * (b + 1))
        K.nc.scalar.activation(scratch[b][0:r], K.X[0:r, b, :], ACT.Square, accum_out=K.ss[0:r, b:b + 1])


def stage_setup(K):
    nc, d = K.nc, K.d
    s_vec, s_x, s_c, s_t, s_v = (K.sem(f"setup_{n}") for n in ("vec", "x", "const", "turn", "out"))
    s_pool, s_br = K.sem("setup_pool"), K.sem("setup_br")
    rows = K.region(A_RING, D)

    with nc.Block() as block:
        @block.sync
        def _(sp):
            sp.dma_start(rows[V_DW:V_DW + W], d["conv_w_dw"][0]).then_inc(s_vec, 16)
            sp.dma_start(rows[V_MIX:V_MIX + 2], d["norm_mix"]).then_inc(s_vec, 16)
            sp.dma_start(rows[V_FFN:V_FFN + 2], d["norm_ffn"]).then_inc(s_vec, 16)
            sp.dma_start(rows[V_B1:V_B1 + 2], d["conv_b_pw1"].rearrange("a (h c) -> (a h) c", h=2)).then_inc(s_vec, 16)
            for r, n in ((V_BDW, "conv_b_dw"), (V_LNG, "conv_ln_g"), (V_LNB, "conv_ln_b")):
                sp.dma_start(rows[r:r + 1], d[n]).then_inc(s_vec, 16)
            sp.dma_start(K.X[:, 0:4, :], d["x_prompt"][0].rearrange("(b p) c -> p b c", p=P)).then_inc(s_x, 16)
            sp.dma_start(K.X[0:NS, 4, :], d["x_sample"].rearrange("s t c -> (s t) c")).then_inc(s_x, 16)
            sp.wait_ge(s_x, 32)

        @block.scalar
        def _(act):
            for i in range(2):
                act.dma_start(K.wr[:, i, :, 0:NG], d["moe_w_coarse"][i].rearrange("(k p) g -> p k g", p=P)).then_inc(s_br, 16)
                for g in range(NG):
                    act.dma_start(K.wr[:, i, :, NG + EPG * g:NG + EPG * (g + 1)],
                                  d["moe_w_fine"][i, g].rearrange("(k p) e -> p k e", p=P)).then_inc(s_br, 16)
                act.dma_start(K.br[:, i, 0:NG], d["moe_b_coarse"][i:i + 1, :].partition_broadcast(P)).then_inc(s_br, 16)
                act.dma_start(K.br[:, i, NG:NR], d["moe_b_fine"][i:i + 1].rearrange("a g e -> a (g e)").partition_broadcast(P)).then_inc(s_br, 16)
            act.wait_ge(s_v, 1)
            act.wait_ge(s_x, 32)
            square_sums(K, act, s_v, 0, [K.region(A_RING + D * (b + 1), D) for b in range(NB)])
            act.wait_ge(s_br, 16 * 2 * (NG + 3))

        @block.gpsimd
        def _(pool):
            chain = Chain(pool, s_pool)
            nc.gpsimd.memset(K.ident[:], 0.0)
            nc.gpsimd.memset(K.before[:], 0.0)
            nc.gpsimd.memset(K.negtri[:], 0.0)
            nc.gpsimd.memset(K.ones[:], 1.0)
            nc.gpsimd.memset(K.negones[:], -1.0)
            chain(nc.gpsimd.memset(K.valid[:], 1.0))
            nc.gpsimd.affine_select(out=K.ident[:], in_=K.ident[:], compare_op=ALU.not_equal, fill=1.0, base=0,
                                    pattern=[[-1, P]], channel_multiplier=1).then_inc(s_c, 1)
            nc.gpsimd.affine_select(out=K.before[:], in_=K.before[:], compare_op=ALU.is_ge, fill=1.0, base=0,
                                    pattern=[[-1, P]], channel_multiplier=1)
            nc.gpsimd.affine_select(out=K.negtri[:], in_=K.negtri[:], compare_op=ALU.is_gt, fill=-1.0, base=0,
                                    pattern=[[1, P]], channel_multiplier=-1)
            nc.gpsimd.affine_select(out=K.valid[:], in_=K.valid[:], compare_op=ALU.is_gt, fill=0.0,
                                    base=NS + P * (NB - 1), pattern=[[-P, NB]], channel_multiplier=-1)
            nc.gpsimd.iota(K.count[:], pattern=[[1, PIECE]], base=0, channel_multiplier=0,
                           allow_small_or_imprecise_dtypes=True)

        @block.vector
        def _(dve):
            nc.vector.memset(K.ss[:], 1.0).then_inc(s_v, 1)
            for k in range(KT):
                dve.wait_ge(s_t, k + 1)
                nc.vector.tensor_copy(K.vec[:, k, :], K.ps[k][:, 0:NV])

        @block.tensor
        def _(pe):
            pe.wait_ge(s_c, 1)
            pe.wait_ge(s_vec, 7 * 16)
            for k in range(KT):
                nc.tensor.transpose(K.ps[k][:, 0:NV], rows[0:NV, k * P:(k + 1) * P], K.ident[0:NV, 0:NV]).then_inc(s_t, 1)


def stage_norm(K, tag, gain_row):
    nc = K.nc
    s_ms, s_rt, s_rs, s_hn, s_t, s_e = (
        K.sem(f"{tag}_{n}") for n in ("mean", "root", "rstd", "scaled", "turned", "out"))
    HN, HT = K.HN(), K.HT()
    small = K.ps[7][:, 0:KT * NS].rearrange("p (k t) -> p k t", k=KT)

    with nc.Block() as block:
        @block.scalar
        def _(act):
            act.wait_ge(s_ms, 1)
            nc.scalar.activation(K.rstd[:], K.ss[:], ACT.Sqrt).then_inc(s_rt, 1)
            act.wait_ge(s_rs, 1)
            for b in (1, 3):
                nc.scalar.activation(HN[:, b, :], K.X[:, b, :], ACT.Copy, scale=K.rstd[:, b:b + 1]).then_inc(s_hn, 1)
            for k in range(1, KT, 2):
                act.wait_ge(s_t, k + 1)
                nc.scalar.activation(HT[:, k, 0:SEQ], K.ps[k % 6][:], ACT.Copy, scale=K.vec[:, k, gain_row:gain_row + 1]).then_inc(s_e, 1)

        @block.vector
        def _(dve):
            nc.vector.tensor_scalar(K.ss[:], K.ss[:], 1.0 / D, NORM_EPS, ALU.mult, ALU.add).then_inc(s_ms, 1)
            dve.wait_ge(s_rt, 1)
            nc.vector.reciprocal(K.rstd[:], K.rstd[:]).then_inc(s_rs, 1)
            dve.wait_ge(s_rs, 1)
            for b in (0, 2, 4):
                r = ROWS[b]
                nc.vector.tensor_scalar(HN[0:r, b, :], K.X[0:r, b, :], K.rstd[0:r, b:b + 1], None, ALU.mult).then_inc(s_hn, 1)
            for k in range(0, KT, 2):
                dve.wait_ge(s_t, k + 1)
                nc.vector.tensor_scalar(HT[:, k, 0:SEQ], K.ps[k % 6][:], K.vec[:, k, gain_row:gain_row + 1], None, ALU.mult).then_inc(s_e, 1)
            dve.wait_ge(s_t, KT)
            nc.vector.tensor_tensor(HT[:, :, SEQ:TOK], small, K.vec[:, :, gain_row:gain_row + 1].to_broadcast([P, KT, NS]), ALU.mult)

        @block.tensor
        def _(pe):
            pe.wait_ge(s_hn, NB)
            for k in range(KT):
                if k >= 6:
                    pe.wait_ge(s_e, KT - 2)
                cols = slice(k * P, (k + 1) * P)
                nc.tensor.transpose(small[:, k, :], HN[0:NS, NB - 1, cols], K.ident[0:NS, 0:NS])
                for b in range(4):
                    last = nc.tensor.transpose(K.ps[k % 6][:, b * P:(b + 1) * P], HN[:, b, cols], K.ident[:])
                last.then_inc(s_t, 1)


def stage_conv_in(K):
    nc, d = K.nc, K.d
    names = ("hist", "histT", "histout", "proj", "sig", "glu", "gchain", "tap", "zero", "prod", "added", "sprod", "sred", "merged")
    s = {n: K.sem(f"conv_{n}") for n in names}
    s_w = [K.sem(f"conv_w{u}") for u in range(2)]
    s_st = K.sem("conv_state_rows")
    s_tr, s_ev, s_out = K.sem("conv_tail_turned"), K.sem("conv_tail_out"), K.sem("conv_state_stored")
    HT = K.HT()
    at = A_XS
    U = K.region(at, KT, STREAM); at += KT * STREAM
    C = K.region(at, KT, TOK); at += KT * TOK
    wt = [K.region(at + u * KT * 2 * P, KT, 2, P) for u in range(2)]; at += 2 * KT * 2 * P
    sg = [K.region(at + u * TOK, TOK) for u in range(2)]; at += 2 * TOK
    hist = K.region(at, 2, D); at += 2 * D
    tail = K.region(at, 2, D); at += 2 * D
    fresh = K.region(at, KT, NS); at += KT * NS
    hn = A_HN
    prods = [K.region(hn + i * SEQ, SEQ) for i in range(3)]; hn += 3 * SEQ
    psum_p = [K.region(hn + i * SEQ, SEQ) for i in range(2)]; hn += 2 * SEQ
    C2 = K.region(hn, SEQ); hn += SEQ
    sprod = K.region(hn, DB, DS, W); hn += DB * DS * W
    sred = [K.region(hn + i * NS, DB, DS, 1) for i in range(2)]; hn += 2 * NS
    assert hn <= A_HT and POOLT % 3 == 0
    K.C = C
    K.w2 = K.region(at, KT, D); at += KT * D
    K.conv_end = at
    K.s_w2 = K.sem("conv_w_pw2")
    wsrc = d["conv_w_pw1"][0].rearrange("(k p) (h c m) -> c p k h m", p=P, h=2, m=P)
    NHR = DB // 2 * HIST
    loops = KT // 2

    def stream(ct, lo, hi):
        return U[:, ct, lo:hi]

    def samples(ct, lo, n):
        return U[:, ct, SAMPLE0:STREAM].rearrange("p (s t) -> p s t", t=HIST + DS)[:, :, lo:lo + n]

    with nc.Block() as block:
        @block.sync
        def _(sp):
            sp.dma_start(hist[0:NHR], d["state_conv"][0].rearrange("(a s) t c -> (s t) a c", a=2)).then_inc(s["hist"], 16)
            sp.dma_start(d["conv_state_s"][0, :, 0:HIST - DS, :], d["state_conv"][0, :, DS:HIST, :]).then_inc(s_st, 16)
            with sp.Fori(0, loops) as it:
                for u in range(2):
                    sp.wait_ge(s["proj"], 2 * it + u + 1)
                    sp.dma_start(wt[u][:, :, 0, :], wsrc[2 * it + u][:, :, 0, :]).then_inc(s_w[u], 16)
                    sp.dma_start(wt[u][:, :, 1, :], wsrc[2 * it + u][:, :, 1, :]).then_inc(s_w[u], 16)
            sp.dma_start(K.w2, d["conv_w_pw2"][0].rearrange("(k p) c -> p k c", p=P)).then_inc(K.s_w2, 16)
            sp.wait_ge(s_st, 16)
            sp.wait_ge(s_ev, 4)
            sp.dma_start(d["conv_state_p"][0, 0], tail[0:HIST, 0, :]).then_inc(s_out, 16)
            for q in range(DB):
                sp.dma_start(d["conv_state_s"][0, q, HIST - DS:HIST, :], tail[DS * q:DS * (q + 1), 1, :]).then_inc(s_out, 16)
            sp.wait_ge(s_out, 16 * (1 + DB))

        @block.gpsimd
        def _(pool):
            nc.gpsimd.memset(U[:, :, 0:HIST], 0.0).then_inc(s["zero"], 1)
            pool.sem_inc(s["added"], POOLT - 1)
            with pool.Fori(0, loops) as it:
                for u in range(2):
                    ct = 2 * it + u
                    pool.wait_ge(s["glu"], ct + 3)
                    pool.wait_ge(s["merged"], ct + 1)
                    win = U[:, bass.ds(ct, 1), :].rearrange("p a c -> p (a c)")[:, SAMPLE0:STREAM]
                    win = bass.AP(win.tensor, win.offset, [win.ap[0], [HIST + DS, DB], [1, DS], [1, W]])
                    taps = K.vec[:, bass.ds(ct, 1), V_DW:V_DW + W].unsqueeze(1).to_broadcast([P, DB, DS, W])
                    nc.gpsimd.tensor_tensor(sprod, win, taps, ALU.mult).then_inc(s["sprod"], 1)
                    for n in range(1, POOLT):
                        pool.wait_ge(s["prod"], POOLT * ct + n + 1)
                        if n > 1:
                            pool.wait_ge(s["added"], (POOLT - 1) * (ct + 1) + n - 1)
                        nc.gpsimd.tensor_tensor(psum_p[u], prods[0] if n == 1 else psum_p[u], prods[n % 3], ALU.add).then_inc(s["added"], 1)
            pool.wait_ge(s["glu"], KT + 2)
            for k in range(KT):
                last = nc.gpsimd.tensor_copy(fresh[:, k, :].rearrange("p (s t) -> p s t", t=DS), samples(k, HIST, DS))
            last.then_inc(s["zero"], 1)

        @block.tensor
        def _(pe):
            pe.wait_ge(s["hist"], 16)
            pe.sem_inc(s["proj"], 2)
            for k in range(KT):
                for a in range(2):
                    last = nc.tensor.transpose(K.ps[k][:, a * NHR:(a + 1) * NHR], hist[0:NHR, a, k * P:(k + 1) * P],
                                               K.ident[0:NHR, 0:NHR])
                last.then_inc(s["histT"], 1)
            pe.wait_ge(s["histout"], KT)
            with pe.Fori(0, loops) as it:
                for u in range(2):
                    pe.wait_ge(s_w[u], 32 * it + 32)
                    pe.wait_ge(s["glu"], 2 * it + u + 1)
                    for h in range(2):
                        for n in range(2):
                            for k in range(KT):
                                last = nc.tensor.matmul(K.ps[4 * u + 2 * h + n][:, 0:HALF], wt[u][:, k, h, :],
                                                        HT[:, k, n * HALF:(n + 1) * HALF], start=(k == 0), stop=(k == KT - 1))
                    last.then_inc(s["proj"], 1)
            pe.wait_ge(s["glu"], KT + 2)
            pe.wait_ge(s["zero"], 2)
            for k in range(KT):
                nc.tensor.transpose(K.ps[k // 4][0:HIST, k % 4 * P:(k % 4 + 1) * P], stream(k, SEQ, SEQ + HIST), K.ident[:])
                last = nc.tensor.transpose(K.ps[2 + k // 4][0:NS, k % 4 * P:(k % 4 + 1) * P], fresh[:, k, :], K.ident[:])
            last.then_inc(s_tr, 1)

        @block.scalar
        def _(act):
            def sigmoid(ct, u):
                act.wait_ge(s["proj"], ct + 3)
                act.wait_ge(s["glu"], ct + 1)
                K.settle(act)
                for n in range(2):
                    last = nc.scalar.activation(sg[u][:, n * HALF:(n + 1) * HALF], K.ps[4 * u + 2 + n][:, 0:HALF],
                                                ACT.Sigmoid, bias=K.vec[:, ct, V_B1 + 1:V_B1 + 2])
                last.then_inc(s["sig"], 1)

            def body(it):
                for u in range(2):
                    ct = 2 * it + u
                    act.wait_ge(s["glu"], ct + 3)
                    for n in range(POOLT):
                        if n == POOLT - 3 and not (isinstance(it, int) and ct == KT - 1):
                            sigmoid(ct + 1, 1 - u)
                        act.wait_ge(s["added"], (POOLT - 1) * (ct + 1) + max(n - 3, 1) if n >= 3 else (POOLT - 1) * ct + n + POOLT - 3)
                        K.settle(act)
                        nc.scalar.activation(prods[n % 3], stream(ct, n, n + SEQ), ACT.Copy, scale=K.vec[:, ct, V_DW + n:V_DW + n + 1]).then_inc(s["prod"], 1)

            sigmoid(0, 0)
            with act.Fori(0, loops - 1) as it:
                body(it)
            body(loops - 1)
            act.wait_ge(s_tr, 1)
            for q in range(4):
                r = HIST if q < 2 else NS
                nc.scalar.activation(tail[0:r, q // 2, q % 2 * 512:(q % 2 + 1) * 512], K.ps[q][0:r, :], ACT.Copy).then_inc(s_ev, 1)

        @block.vector
        def _(dve):
            dve.sem_inc(s["glu"], 2)
            for k in range(KT):
                dve.wait_ge(s["histT"], k + 1)
                nc.vector.tensor_copy(samples(k, 0, HIST), K.ps[k][:, 0:2 * NHR].rearrange("p (s t) -> p s t", t=HIST)).then_inc(s["histout"], 1)
            dve.wait_ge(s["zero"], 1)
            dve.wait_ge(s["histout"], KT)
            dve.sem_inc(s["merged"], 2)
            taps = W - POOLT + 2

            def merge(ct, u):
                dve.wait_ge(s["added"], (POOLT - 1) * (ct + 2))
                dve.wait_ge(s["tap"], taps * ct + W - POOLT + 1)
                c = C[:, ct, 0:SEQ]
                nc.vector.tensor_tensor(c, c, psum_p[u], ALU.add).then_inc(s["merged"], 1)

            def body(it):
                for u in range(2):
                    ct = 2 * it + u
                    dve.wait_ge(s["sig"], ct + 1)
                    ba = K.vec[:, ct, V_B1:V_B1 + 1]
                    nc.vector.scalar_tensor_tensor(out=stream(ct, HIST, HIST + HALF), in0=K.ps[4 * u][:, 0:HALF], scalar=ba,
                                                   in1=sg[u][:, 0:HALF], op0=ALU.add, op1=ALU.mult)
                    nc.vector.scalar_tensor_tensor(out=stream(ct, HIST + HALF, HIST + SEQ), in0=K.ps[4 * u + 1][:, 0:SEQ - HALF], scalar=ba,
                                                   in1=sg[u][:, HALF:SEQ], op0=ALU.add, op1=ALU.mult)
                    nc.vector.scalar_tensor_tensor(
                        out=samples(ct, HIST, DS), in0=K.ps[4 * u + 1][:, SEQ - HALF:HALF].rearrange("p (s t) -> p s t", t=DS), scalar=ba,
                        in1=sg[u][:, SEQ:TOK].rearrange("p (s t) -> p s t", t=DS), op0=ALU.add, op1=ALU.mult).then_inc(s["gchain"], 1)
                    dve.wait_ge(s["gchain"], ct + 1)
                    dve.sem_inc(s["glu"], 1)
                    if not (isinstance(it, int) and ct == 0):
                        dve.wait_ge(s["tap"], taps * ct)
                    bd = K.vec[:, ct, V_BDW:V_BDW + 1]
                    c = C[:, ct, 0:SEQ]
                    for n, j in enumerate(range(POOLT, W)):
                        wj, x = K.vec[:, ct, V_DW + j:V_DW + j + 1], stream(ct, j, j + SEQ)
                        if n >= 2:
                            dve.wait_ge(s["tap"], taps * ct + n - 1)
                        if n == 0:
                            last = nc.vector.tensor_scalar(c, x, wj, bd, ALU.mult, ALU.add)
                        elif n == 1:
                            last = nc.vector.tensor_scalar(C2, x, wj, None, ALU.mult)
                        else:
                            y = C2 if n % 2 else c
                            last = nc.vector.scalar_tensor_tensor(out=y, in0=x, scalar=wj, in1=y, op0=ALU.mult, op1=ALU.add)
                        last.then_inc(s["tap"], 1)
                        if j == POOLT + 7 and not (isinstance(it, int) and ct == 0):
                            merge(ct - 1, 1 - u)
                    n = W - POOLT
                    dve.wait_ge(s["tap"], taps * ct + n)
                    nc.vector.tensor_tensor(c, c, C2, ALU.add).then_inc(s["tap"], 1)
                    dve.wait_ge(s["sprod"], ct + 1)
                    nc.vector.tensor_reduce(sred[u], sprod, AX.X, ALU.add).then_inc(s["sred"], 1)
                    dve.wait_ge(s["sred"], ct + 1)
                    nc.vector.tensor_scalar(C[:, ct, SEQ:TOK], sred[u].rearrange("p s t o -> p (s t o)"), bd, None, ALU.add).then_inc(s["tap"], 1)

            body(0)
            with dve.Fori(1, loops) as it:
                body(it)
            merge(KT - 1, 1)


def stage_conv_out(K):
    nc, d = K.nc, K.d
    names = ("sum", "mean", "centred", "square", "sumsq", "var", "root", "rstd", "scaled", "act", "y", "added", "bias", "b2")
    s = {n: K.sem(f"convout_{n}") for n in names}
    C = K.C
    at = K.conv_end
    sq = K.region(at, KT, TOK); at += KT * TOK
    mean, rstd = K.region(A_HT, TOK), K.region(A_HT + TOK, TOK)
    halves = [slice(0, HALF), slice(HALF, TOK)]

    with nc.Block() as block:
        @block.sync
        def _(sp):
            sp.wait_ge(s["b2"], 16)

        @block.gpsimd
        def _(pool):
            b2 = K.region(A_HN, D)
            pool.dma_start(b2, d["conv_b_pw2"].partition_broadcast(P)).then_inc(s["b2"], 16)
            pool.wait_ge(s["b2"], 16)
            for b, r in enumerate(ROWS):
                last = nc.gpsimd.tensor_tensor(K.X[0:r, b, :], K.X[0:r, b, :], b2[0:r], ALU.add)
            last.then_inc(s["bias"], 1)

        @block.tensor
        def _(pe):
            for h in range(2):
                for k in range(KT):
                    last = nc.tensor.matmul(K.ps[h][:, 0:HALF], K.ones[:], C[:, k, halves[h]], start=(k == 0), stop=(k == KT - 1))
            last.then_inc(s["sum"], 1)
            for k in range(KT):
                pe.wait_ge(s["square"], k + 1)
                for h in range(2):
                    last = nc.tensor.matmul(K.ps[2 + h][:, 0:HALF], K.ones[:], sq[:, k, halves[h]], start=(k == 0), stop=(k == KT - 1))
            last.then_inc(s["sumsq"], 1)
            pe.wait_ge(K.s_w2, 16)
            for b, r in enumerate(ROWS):
                for n in range(2):
                    g = 2 * b + n
                    if g >= 4:
                        pe.wait_ge(s["added"], g - 3)
                    for k in range(KT):
                        if g == 0:
                            pe.wait_ge(s["act"], k + 1)
                        last = nc.tensor.matmul(K.ps[4 + g % 4][0:r, :], C[:, k, b * P:b * P + r], K.w2[:, k, n * 512:(n + 1) * 512],
                                                start=(k == 0), stop=(k == KT - 1))
                    last.then_inc(s["y"], 1)

        @block.scalar
        def _(act):
            for k in range(KT):
                act.wait_ge(s["centred"], k + 1)
                nc.scalar.activation(sq[:, k, :], C[:, k, :], ACT.Square).then_inc(s["square"], 1)
            act.wait_ge(s["var"], 1)
            nc.scalar.activation(rstd, rstd, ACT.Sqrt).then_inc(s["root"], 1)
            for k in range(KT):
                act.wait_ge(s["scaled"], k + 1)
                nc.scalar.activation(C[:, k, :], C[:, k, :], ACT.Silu, bias=K.vec[:, k, V_LNB:V_LNB + 1],
                                     scale=K.vec[:, k, V_LNG:V_LNG + 1]).then_inc(s["act"], 1)
            square_sums(K, act, s["added"], 2, [K.region(A_HT + 2 * TOK, D)] + [K.region(A_HN + D * b, D) for b in range(1, NB)])

        @block.vector
        def _(dve):
            dve.wait_ge(s["sum"], 1)
            for h in range(2):
                last = nc.vector.tensor_scalar(mean[:, halves[h]], K.ps[h][:, 0:HALF], 1.0 / D, None, ALU.mult)
            last.then_inc(s["mean"], 1)
            dve.wait_ge(s["mean"], 1)
            for k in range(KT):
                nc.vector.tensor_tensor(C[:, k, :], C[:, k, :], mean, ALU.subtract).then_inc(s["centred"], 1)
            dve.wait_ge(s["sumsq"], 1)
            for h in range(2):
                last = nc.vector.tensor_scalar(rstd[:, halves[h]], K.ps[2 + h][:, 0:HALF], 1.0 / D, LN_EPS, ALU.mult, ALU.add)
            last.then_inc(s["var"], 1)
            dve.wait_ge(s["root"], 1)
            nc.vector.reciprocal(rstd, rstd).then_inc(s["rstd"], 1)
            dve.wait_ge(s["rstd"], 1)
            for k in range(KT):
                dve.wait_ge(s["square"], k + 1)
                nc.vector.tensor_tensor(C[:, k, :], C[:, k, :], rstd, ALU.mult).then_inc(s["scaled"], 1)
            dve.wait_ge(s["bias"], 1)
            for b, r in enumerate(ROWS):
                for n in range(2):
                    g = 2 * b + n
                    dve.wait_ge(s["y"], g + 1)
                    x = K.X[0:r, b, n * 512:(n + 1) * 512]
                    nc.vector.tensor_tensor(x, x, K.ps[4 + g % 4][0:r, :], ALU.add).then_inc(s["added"], 1)


def load_in(K, sp, layer, e, u, sem):
    for m, name in enumerate(("moe_w_gate", "moe_w_up")):
        sp.dma_start(K.region(A_RING + u * EW + m * KT * FE, KT, FE), K.d[name][layer, e].rearrange("(k p) f -> p k f", p=P)).then_inc(sem, 16)


def load_down(K, sp, layer, e, u, sem):
    sp.dma_start(K.region(A_RING + u * EW + 2 * KT * FE, FE // P, D), K.d["moe_w_down"][layer, e].rearrange("(j p) c -> p j c", p=P)).then_inc(sem, 16)


def late_places(K):
    dims = ((NB, NG + 1), (NB, 1), (NB, 1), (NB, 1), (NE,), (NE + 2,), (1,), (RING,))
    at, views = A_RING - 256, []
    for dim in dims:
        views.append(K.region(at, *dim))
        at += int(np.prod(dim))
    assert at <= A_RING
    return views


def first_slots(K, do):
    v = K.nc.vector
    st, early = late_places(K)[5], late_places(K)[7]
    v.tensor_copy(K.start[:], st)
    do(v.tensor_scalar(early, K.iota[:, 0:RING], float(CAP), None, ALU.mult))
    do(v.tensor_tensor(early, early, st[:, 0:RING], ALU.min))
    return v.tensor_copy(K.early[:], early)


def late_results(K, do):
    v = K.nc.vector
    ex, esum, gtop, w1, cnt, st, mx, _ = late_places(K)
    do(v.tensor_reduce(esum, ex[:, :, 0:NG], AX.X, ALU.add))
    do(v.reciprocal(gtop, esum))
    do(v.tensor_scalar(w1, ex[:, :, NG:NG + 1], 1.0, None, ALU.add))
    do(v.reciprocal(w1, w1))
    do(v.tensor_tensor(K.wts[:, :, 0:1], gtop, w1, ALU.mult))
    do(v.tensor_tensor(K.wts[:, :, 1:2], K.wts[:, :, 0:1], ex[:, :, NG:NG + 1], ALU.mult))
    for c in range(NPASS):
        v.tensor_scalar(K.starts[:].rearrange("p (e c) -> p e c", c=NPASS)[:, :, c], st[:, 0:NE], float(c * CAP), float(SLOTS), ALU.add, ALU.min)
    do(v.tensor_reduce(mx, cnt, AX.X, ALU.max))
    do(v.tensor_scalar(mx, mx, float(CAP), None, ALU.is_gt))
    do(v.tensor_copy(K.over[:], mx))


def stage_route(K, layer):
    nc = K.nc
    K.s_win = [K.sem(f"moe{layer}_win{w}") for w in range(2)]
    K.s_wdown = [K.sem(f"moe{layer}_wdown{w}") for w in range(2)]
    s_part, s_rest = K.sem(f"route{layer}_part"), K.sem(f"route{layer}_rest")
    HN, part = K.HN(), [K.part(i) for i in range(3)]
    names = ("logits", "member", "rank", "exp", "chain", "pool")
    s = {n: K.sem(f"route{layer}_{n}") for n in names}
    HT = K.HT()
    at = [A_XS]

    def tmp(*dims):
        n = 1
        for x in dims:
            n *= x
        v = K.region(at[0], *dims)
        at[0] += n
        return v

    lg = tmp(NB, NR)
    c8, cm, f8, fm = (tmp(NB, 8) for _ in range(4))
    ci, fi = (tmp(NB, 8).bitcast(U32) for _ in range(2))
    og = tmp(NB, NG)
    prod = tmp(NB, NG, EPG)
    gi, fidx, e1, e2 = (tmp(NB, 1) for _ in range(4))
    m1, m2, rk, t1 = (tmp(NB, NE) for _ in range(4))
    scan, zero = (tmp(NE) for _ in range(2))
    ex, _, _, _, cnt, st, _, _ = late_places(K)
    REST = tmp(NB, D)
    first = K.region16(at[0], NB, D); tmp(NB * D // 2)
    before, ones = (tmp(P // 2).bitcast(BF16) for _ in range(2))
    mm = tmp(NB, NE // 2)
    mm = K.region16(at[0] - NB * NE // 2, NB, NE)
    logits = K.ps[0][:, 0:NB * NR].rearrange("p (b r) -> p b r", b=NB)
    ranks = K.ps[1][:, 0:NB * NE].rearrange("p (b r) -> p b r", b=NB)
    counts = K.ps[2][:, 0:NE]

    with nc.Block() as block:
        @block.tensor
        def _(pe):
            for b, r in enumerate(ROWS):
                for k in range(KT):
                    last = nc.tensor.matmul(logits[0:r, b, :], HT[:, k, b * P:b * P + r], K.wr[:, layer, k, :], start=(k == 0), stop=(k == KT - 1))
            last.then_inc(s["logits"], 1)
            pe.wait_ge(s["pool"], 1)
            pe.wait_ge(s["member"], 1)
            for b in range(NB):
                for b2 in range(b + 1):
                    nc.tensor.matmul(ranks[:, b, :], before if b2 == b else ones, mm[:, b2, :], start=(b2 == 0), stop=(b2 == b))
            for b in range(NB):
                last = nc.tensor.matmul(counts, ones, mm[:, b, :], start=(b == 0), stop=(b == NB - 1))
            last.then_inc(s["rank"], 1)

        @block.sync
        def _(sp):
            for w in range(2):
                for u in (2 * w, 2 * w + 1):
                    load_in(K, sp, layer, u, u, K.s_win[w])
                for u in (2 * w, 2 * w + 1):
                    load_down(K, sp, layer, u, u, K.s_wdown[w])

        @block.gpsimd
        def _(pool):
            nc.gpsimd.tensor_copy(before, K.before[:])
            nc.gpsimd.tensor_copy(ones, K.ones[:]).then_inc(s["pool"], 1)
            for i in range(2):
                if i == 1:
                    pool.wait_ge(s_rest, NB)
                for b, rr in enumerate(ROWS):
                    pool.wait_ge(s_part, NB * i + b + 1)
                    whole, rest = ((HN, REST), (REST, part[2]))[i]
                    nc.gpsimd.tensor_tensor(rest[0:rr, b, :], whole[0:rr, b, :], (first, part[1])[i][0:rr, b, :], ALU.subtract).then_inc(s_rest, 1)

        @block.scalar
        def _(act):
            for i in range(2):
                for b, rr in enumerate(ROWS):
                    if i == 1:
                        act.wait_ge(s_rest, b + 1)
                    nc.scalar.activation((first, part[1])[i][0:rr, b, :], (HN, REST)[i][0:rr, b, :], ACT.Copy).then_inc(s_part, 1)
            act.wait_ge(s["logits"], 1)
            act.wait_ge(s_part, NB)
            for b, rr in enumerate(ROWS):
                nc.scalar.activation(part[0][0:rr, b, :], first[0:rr, b, :], ACT.Copy)
            act.wait_ge(s["exp"], 1)
            nc.scalar.activation(ex, ex, ACT.Exp)

        @block.vector
        def _(dve):
            do = Chain(dve, s["chain"])
            v = nc.vector
            v.memset(lg, 0.0)
            v.memset(zero, 1.0)
            v.memset(st, float(SLOTS))
            do(v.memset(c8, NEG))
            dve.wait_ge(s["logits"], 1)
            br = K.br[:, layer, :]
            v.tensor_tensor(lg[:, 0:NB - 1, :], logits[:, 0:NB - 1, :], br.unsqueeze(1).to_broadcast([P, NB - 1, NR]), ALU.add)
            do(v.tensor_tensor(lg[0:NS, NB - 1, :], logits[0:NS, NB - 1, :], br[0:NS], ALU.add))
            do(v.tensor_copy(c8[:, :, 0:NG], lg[:, :, 0:NG]))
            for b in range(NB):
                last = v.max(cm[:, b, :], c8[:, b, :])
            do(last)
            for b in range(NB):
                last = v.max_index(ci[:, b, :], cm[:, b, :], c8[:, b, :])
            do(last)
            do(v.tensor_copy(gi, ci[:, :, 0:1]))
            do(v.tensor_tensor(og, K.iota[:, 0:NG].unsqueeze(1).to_broadcast([P, NB, NG]), gi.to_broadcast([P, NB, NG]), ALU.is_equal))
            for g in range(NG):
                last = v.tensor_tensor(prod[:, :, g, :], lg[:, :, NG + EPG * g:NG + EPG * (g + 1)],
                                       og[:, :, g:g + 1].to_broadcast([P, NB, EPG]), ALU.mult)
            do(last)
            do(v.tensor_reduce(f8, prod.rearrange("p b g e -> p b e g"), AX.X, ALU.add))
            for b in range(NB):
                last = v.max(fm[:, b, :], f8[:, b, :])
            do(last)
            for b in range(NB):
                last = v.max_index(fi[:, b, :], fm[:, b, :], f8[:, b, :])
            do(last)
            for j, e in ((0, e1), (1, e2)):
                do(v.tensor_copy(fidx, fi[:, :, j:j + 1]))
                do(v.scalar_tensor_tensor(out=e, in0=gi, scalar=float(EPG), in1=fidx, op0=ALU.mult, op1=ALU.add))
            for m, e in ((m1, e1), (m2, e2)):
                do(v.tensor_tensor(m, K.iota.unsqueeze(1).to_broadcast([P, NB, NE]), e.to_broadcast([P, NB, NE]), ALU.is_equal))
                do(v.tensor_tensor(m, m, K.valid[:].unsqueeze(2).to_broadcast([P, NB, NE]), ALU.mult))
            v.tensor_tensor(mm, m1, m2, ALU.add).then_inc(s["member"], 1)
            v.tensor_tensor(ex[:, :, 0:NG], lg[:, :, 0:NG], cm[:, :, 0:1].to_broadcast([P, NB, NG]), ALU.subtract)
            v.tensor_tensor(ex[:, :, NG:NG + 1], fm[:, :, 1:2], fm[:, :, 0:1], ALU.subtract).then_inc(s["exp"], 1)
            dve.wait_ge(s["rank"], 1)
            do(v.tensor_copy(cnt, counts))
            do(v.tensor_tensor_scan(scan, zero, cnt, 0.0, ALU.mult, ALU.add))
            do(v.tensor_tensor(st[:, 0:NE], scan, cnt, ALU.subtract))
            do(v.tensor_tensor(rk, ranks, st[:, 0:NE].unsqueeze(1).to_broadcast([P, NB, NE]), ALU.add))
            for j, m in ((0, m1), (1, m2)):
                do(v.tensor_tensor(t1, rk, m, ALU.mult))
                do(v.tensor_reduce(K.posf[:, 0, :, j:j + 1], t1, AX.X, ALU.add))
            v.tensor_copy(K.pos[:], K.posf[:, 0])
            for i in range(1, len(PIECES)):
                last = v.tensor_scalar(K.posf[:, i], K.posf[:, 0], -float(PIECES[i][0]), None, ALU.add)
            do(last)


def stage_moe(K, layer):
    nc, d = K.nc, K.d
    L = f"moe{layer}_"
    names = ("pad", "padded", "picked", "turned", "xa", "xv", "chain")
    s = {n: K.sem(L + n) for n in names}
    NJ = FE // P
    XT = K.region(A_XS, KT, XCOLS)
    at = A_HN
    xe = [K.region(at + w * 2 * KT * CAP, KT, 2, CAP) for w in range(2)]; at += 4 * KT * CAP
    gs, h, hT = (K.region(at + i * FE, NJ, P) for i in range(3)); at += 3 * FE
    yo = [K.region(at + w * D, KT, P) for w in range(2)]; at += 2 * D
    late = (xe, gs, h, hT, yo)
    o = PIECE
    xe = [XT[:, :, o + w * 2 * CAP:o + (w + 1) * 2 * CAP].rearrange("p k (q t) -> p k q t", q=2) for w in range(2)]
    o += 4 * CAP
    gs, h, hT = (XT[:, i * NJ:(i + 1) * NJ, o:o + P] for i in range(3))
    o = SLOTS - 2 * P
    yo = [XT[:, :, o + w * P:o + (w + 1) * P] for w in range(2)]
    early = (xe, gs, h, hT, yo)
    assert PIECE + 4 * CAP + P <= o and PIECES[2][0] <= o and RING * CAP <= PIECE
    wg, wu, wd = [], [], []
    for u in range(RING):
        o = A_RING + u * EW
        wg.append(K.region(o, KT, FE))
        wu.append(K.region(o + KT * FE, KT, FE))
        wd.append(K.region(o + 2 * KT * FE, NJ, D))
    gain = V_FFN + layer
    iters = NE // RING
    reg = lambda eng, ap, hi: eng.value_load(ap, min_val=0, max_val=hi)
    half = (slice(0, CAP), slice(CAP, 2 * CAP))

    def project(m, us, xe):
        for k in range(KT):
            for q, u in enumerate(us):
                last = nc.tensor.matmul(K.ps[m][half[q], 0:FE], xe[:, k, q, :], (wg, wu)[m][u][:, k, :], start=(k == 0), stop=(k == KT - 1))
        return last

    def turn(h):
        for j in range(NJ):
            last = nc.tensor.transpose(K.ps[2][:, j * P:(j + 1) * P], h[:, j, :], K.ident[:])
        return last

    def down(us, v, hT):
        for n in range(2):
            for j in range(NJ):
                for q, u in enumerate(us):
                    last = nc.tensor.matmul(K.ps[4 + 2 * v + n][half[q], :], hT[:, j, half[q]], wd[u][:, j, n * 512:(n + 1) * 512],
                                            start=(j == 0), stop=(j == NJ - 1))
        return last

    flat = lambda t: t.rearrange("p (j t) -> p j t", t=P)

    names = ("start", "in", "gate", "up", "silu", "h", "ht", "hT", "y", "ya", "yv", "store")
    es = {n: K.sem(L + "pair_" + n) for n in names}

    def pair_pe(pe, it, g, w, bufs, first):
        xe, gs, h, hT, yo = bufs
        us = (2 * w, 2 * w + 1)
        pe.wait_ge(K.s_win[w], 64 * it + 64)
        pe.wait_ge(es["in"], 2 * g + 2)
        project(0, us, xe[w]).then_inc(es["gate"], 1)
        project(1, us, xe[w]).then_inc(es["up"], 1)
        pe.wait_ge(es["h"], g + 1)
        K.settle(pe)
        turn(h).then_inc(es["ht"], 1)
        pe.wait_ge(K.s_wdown[w], 32 * it + 32)
        pe.wait_ge(es["hT"], g + 1)
        if not first:
            pe.wait_ge(es["ya"], g - 1)
            pe.wait_ge(es["yv"], g - 1)
        down(us, w, hT).then_inc(es["y"], 1)

    def pair_act(act, g, w, bufs, first):
        xe, gs, h, hT, yo = bufs
        act.wait_ge(es["gate"], g + 1)
        if not (first and g == 0):
            act.wait_ge(es["h"], g)
        nc.scalar.activation(gs, flat(K.ps[0][:, 0:FE]), ACT.Silu).then_inc(es["silu"], 1)
        act.wait_ge(es["y"], g + 1)
        if not first:
            act.wait_ge(es["store"], 32 * g - 32)
        nc.scalar.activation(yo[w][:, 0:KT // 2], flat(K.ps[4 + 2 * w][:]), ACT.Copy).then_inc(es["ya"], 1)

    def pair_slots(dve, g, w, bufs, first):
        for q in range(2):
            e = 2 * g + q
            st = reg(dve, K.early[0:1, e:e + 1], CAP * (RING - 1)) if first else reg(dve, K.start[0:1, bass.ds(e, 1)], SLOTS)
            if not first:
                dve.wait_ge(es["up"], g - 1)
            nc.vector.tensor_copy(bufs[0][w][:, :, q], XT[:, :, bass.ds(st, CAP)]).then_inc(es["in"], 1)

    def pair_dve(dve, g, w, bufs, first):
        xe, gs, h, hT, yo = bufs
        dve.wait_ge(es["silu"], g + 1)
        dve.wait_ge(es["up"], g + 1)
        nc.vector.tensor_tensor(h, gs, flat(K.ps[1][:, 0:FE]), ALU.mult).then_inc(es["h"], 1)
        dve.wait_ge(es["ht"], g + 1)
        nc.vector.tensor_copy(hT, flat(K.ps[2][:, 0:FE])).then_inc(es["hT"], 1)
        dve.wait_ge(es["y"], g + 1)
        if not first:
            dve.wait_ge(es["store"], 32 * g - 32)
        nc.vector.tensor_copy(yo[w][:, KT // 2:KT], flat(K.ps[5 + 2 * w][:])).then_inc(es["yv"], 1)

    def pair_stores(pool, g, w, bufs, first):
        for q in range(2):
            e = 2 * g + q
            st = reg(pool, K.start[0:1, bass.ds(e, 1)], SLOTS)
            pool.wait_ge(es["ya"], g + 1)
            pool.wait_ge(es["yv"], g + 1)
            if not (first and e == 0):
                pool.wait_ge(es["store"], 16 * e)
            pool.dma_start(K.ys_dram[bass.ds(st, CAP), :].rearrange("r (k c) -> r k c", c=P), bufs[4][w][half[q]]).then_inc(es["store"], 16)

    def pair_weights(sp, g, w):
        sp.wait_ge(es["up"], g - 1)
        for q in range(2):
            load_in(K, sp, layer, 2 * g + q, 2 * w + q, K.s_win[w])
        sp.wait_ge(es["y"], g - 1)
        for q in range(2):
            load_down(K, sp, layer, 2 * g + q, 2 * w + q, K.s_wdown[w])

    pick = [K.region16(A_PICK + i * NB * PIECE // 2, NB, PIECE) for i in range(2)]
    parts = [K.part(i) for i in range(3)]
    groups = [(i, m) for i in range(len(PIECES)) for m in range(KT)]
    with nc.Block() as block:
        @block.gpsimd
        def _(pool):
            nc.gpsimd.memset(XT[:, :, SLOTS:XCOLS], 0.0).then_inc(s["pad"], 1)
            pool.wait_ge(es["start"], 1)
            for g in range(2):
                pair_stores(pool, g, g, early, True)

        @block.sync
        def _(sp):
            sp.wait_ge(s["pad"], 1)
            sp.dma_start(K.ys_dram.rearrange("r c -> (r c)")[SLOTS * D:XCOLS * D].rearrange("(p k c) -> p k c", p=P, k=KT), XT[:, :, SLOTS:XCOLS]).then_inc(s["padded"], 16)
            for g in (2, 3):
                pair_weights(sp, g, g - 2)
            sp.wait_ge(s["padded"], 16)

        @block.tensor
        def _(pe):
            for t, (i, m) in enumerate(groups):
                n = PIECES[i][1]
                if t == KT:
                    pe.wait_ge(s["xa"], KT // 2)
                    for g in range(2):
                        pair_pe(pe, 0, g, g, early, True)
                    pe.wait_ge(es["ya"], 2)
                    pe.wait_ge(es["yv"], 2)
                if m == 0:
                    pe.wait_ge(s["picked"], NB * (i + 1))
                if t >= 8:
                    pe.wait_ge(s[("xa", "xv")[t % 2]], (t - 8) // 2 + 1)
                for b, rr in enumerate(ROWS):
                    for c, part in enumerate(parts):
                        last = nc.tensor.matmul(K.ps[t % 8][:, 0:n], part[0:rr, b, m * P:(m + 1) * P], pick[i % 2][0:rr, b, 0:n],
                                                start=(b == 0 and c == 0), stop=(b == NB - 1 and c == 2))
                last.then_inc(s["turned"], 1)

        def columns_out(eng, t, scaled):
            i, m = groups[t]
            o, n = PIECES[i]
            eng.wait_ge(s["turned"], t + 1)
            scaled(XT[:, m, o:o + n], K.ps[t % 8][:, 0:n], K.vec[:, m, gain:gain + 1]).then_inc(s[("xa", "xv")[t % 2]], 1)

        @block.scalar
        def _(act):
            for t in range(0, len(groups), 2):
                if t == KT:
                    for g in range(2):
                        pair_act(act, g, g, early, True)
                if t == 2 * KT:
                    act.wait_ge(es["store"], 64)
                columns_out(act, t, lambda out, i, g: nc.scalar.activation(out, i, ACT.Copy, scale=g))

        @block.vector
        def _(dve):
            do = Chain(dve, s["chain"])

            def one_hot(i):
                n = PIECES[i][1]
                if i >= 2:
                    dve.wait_ge(s["turned"], KT * (i - 1))
                for b in range(NB):
                    last = nc.vector.tensor_scalar(pick[i % 2][:, b, 0:n], K.count[:, 0:n], K.posf[:, i, b, 0:1], None, ALU.is_equal)
                do(last)
                for b in range(NB):
                    nc.vector.scalar_tensor_tensor(out=pick[i % 2][:, b, 0:n], in0=K.count[:, 0:n], scalar=K.posf[:, i, b, 1:2],
                                                   in1=pick[i % 2][:, b, 0:n], op0=ALU.is_equal, op1=ALU.add).then_inc(s["picked"], 1)

            one_hot(0)
            one_hot(1)
            first_slots(K, do).then_inc(es["start"], 1)
            for t in range(1, len(groups), 2):
                if t == KT + 1:
                    dve.wait_ge(s["xa"], KT // 2)
                    dve.wait_ge(s["xv"], KT // 2)
                    dve.wait_ge(es["start"], 1)
                    for g in range(2):
                        pair_slots(dve, g, g, early, True)
                    for g in range(2):
                        pair_dve(dve, g, g, early, True)
                    late_results(K, do)
                    one_hot(2)
                if t == 2 * KT + 1:
                    dve.wait_ge(es["store"], 64)
                columns_out(dve, t, lambda out, i, g: nc.vector.tensor_scalar(out, i, g, None, ALU.mult))

    with nc.Block() as block:
        @block.sync
        def _(sp):
            with sp.Fori(2, iters) as it:
                for w in range(2):
                    pair_weights(sp, 2 * it + w, w)

        @block.tensor
        def _(pe):
            with pe.Fori(1, iters) as it:
                for w in range(2):
                    pair_pe(pe, it, 2 * it + w, w, late, False)

        @block.scalar
        def _(act):
            with act.Fori(1, iters) as it:
                for w in range(2):
                    pair_act(act, 2 * it + w, w, late, False)

        @block.vector
        def _(dve):
            pair_slots(dve, 2, 0, late, False)
            with dve.Fori(1, iters) as it:
                for w in range(2):
                    pair_slots(dve, 2 * it + w + 1, 1 - w, late, False)
                    pair_dve(dve, 2 * it + w, w, late, False)

        @block.gpsimd
        def _(pool):
            with pool.Fori(1, iters) as it:
                for w in range(2):
                    pair_stores(pool, 2 * it + w, w, late, False)
            pool.wait_ge(es["store"], 16 * NE)

    names = ("in", "gate", "up", "silu", "h", "ht", "hT", "y", "ya", "yv", "store", "stored")
    r = {n: K.sem(f"{L}all_{n}") for n in names}
    turns = NPASS // 2
    xe, gs, h, hT, yo = late
    with nc.Block() as block:
        @block.sync
        def _(sp):
            flag = reg(sp, K.over[0:1, 0:1], 1)
            with sp.If(flag > 0):
                with sp.Fori(0, NE) as e:
                    sp.wait_ge(r["y"], turns * e + 1)
                    load_in(K, sp, layer, e, 0, K.s_win[0])
                    load_down(K, sp, layer, e, 0, K.s_wdown[0])

        @block.tensor
        def _(pe):
            flag = reg(pe, K.over[0:1, 0:1], 1)
            with pe.If(flag > 0):
                pe.sem_inc(r["y"], 1)
                with pe.Fori(0, NE) as e:
                    with pe.Fori(0, turns) as c:
                        n = turns * e + c
                        pe.wait_ge(K.s_win[0], 64 * iters + 32 * e + 32)
                        pe.wait_ge(K.s_wdown[0], 32 * iters + 16 * e + 16)
                        pe.wait_ge(r["in"], 2 * n + 2)
                        project(0, (0, 0), xe[0]).then_inc(r["gate"], 1)
                        project(1, (0, 0), xe[0]).then_inc(r["up"], 1)
                        pe.wait_ge(r["h"], n + 2)
                        K.settle(pe)
                        turn(h).then_inc(r["ht"], 1)
                        pe.wait_ge(r["hT"], n + 1)
                        pe.wait_ge(r["ya"], n + 1)
                        pe.wait_ge(r["yv"], n + 1)
                        down((0, 0), 0, hT).then_inc(r["y"], 1)

        @block.scalar
        def _(act):
            flag = reg(act, K.over[0:1, 0:1], 1)
            with act.If(flag > 0):
                act.sem_inc(r["ya"], 1)
                with act.Fori(0, NE * turns) as n:
                    act.wait_ge(r["gate"], n + 1)
                    act.wait_ge(r["h"], n + 1)
                    nc.scalar.activation(gs, flat(K.ps[0][:, 0:FE]), ACT.Silu).then_inc(r["silu"], 1)
                    act.wait_ge(r["y"], n + 2)
                    act.wait_ge(r["stored"], n + 1)
                    nc.scalar.activation(yo[0][:, 0:KT // 2], flat(K.ps[4][:]), ACT.Copy).then_inc(r["ya"], 1)

        @block.vector
        def _(dve):
            flag = reg(dve, K.over[0:1, 0:1], 1)
            with dve.If(flag > 0):
                dve.sem_inc(r["yv"], 1)
                dve.sem_inc(r["h"], 1)
                with dve.Fori(0, NE * turns) as n:
                    for q in range(2):
                        st = reg(dve, K.starts[0:1, bass.ds(2 * n + q, 1)], SLOTS)
                        dve.wait_ge(r["y"], n + 1)
                        nc.vector.tensor_copy(xe[0][:, :, q], XT[:, :, bass.ds(st, CAP)]).then_inc(r["in"], 1)
                    dve.wait_ge(r["silu"], n + 1)
                    dve.wait_ge(r["up"], n + 1)
                    nc.vector.tensor_tensor(h, gs, flat(K.ps[1][:, 0:FE]), ALU.mult).then_inc(r["h"], 1)
                    dve.wait_ge(r["ht"], n + 1)
                    nc.vector.tensor_copy(hT, flat(K.ps[2][:, 0:FE])).then_inc(r["hT"], 1)
                    dve.wait_ge(r["y"], n + 2)
                    dve.wait_ge(r["stored"], n + 1)
                    nc.vector.tensor_copy(yo[0][:, KT // 2:KT], flat(K.ps[5][:])).then_inc(r["yv"], 1)

        @block.gpsimd
        def _(pool):
            flag = reg(pool, K.over[0:1, 0:1], 1)
            with pool.If(flag > 0):
                pool.sem_inc(r["stored"], 1)
                with pool.Fori(0, NE * turns) as n:
                    for q in range(2):
                        st = reg(pool, K.starts[0:1, bass.ds(2 * n + q, 1)], SLOTS)
                        pool.wait_ge(r["ya"], n + 2)
                        pool.wait_ge(r["yv"], n + 2)
                        pool.dma_start(K.ys_dram[bass.ds(st, CAP), :].rearrange("r (k c) -> r k c", c=P), yo[0][half[q]]).then_inc(r["store"], 16)
                        pool.wait_ge(r["store"], 32 * n + 16 * q + 16)
                    pool.sem_inc(r["stored"], 1)

    s_g = [K.sem(f"{L}rows_back{b}") for b in range(NB)]
    s_c = K.sem(L + "sum")
    Y = K.region(A_HN, NB, 2, D)
    with nc.Block() as block:
        @block.gpsimd
        def _(pool):
            for b, rr in enumerate(ROWS):
                for j in range(2):
                    pool.indirect_dma_start(Y[0:rr, b, j, :], None, K.ys_dram, bass.IndirectOffsetOnAxis(ap=K.pos[0:rr, b, j:j + 1], axis=0)).then_inc(s_g[b], 16)

        @block.scalar
        def _(act):
            square_sums(K, act, s_c, 2, [K.region(A_RING + D * b, D) for b in range(NB)])

        @block.vector
        def _(dve):
            do = Chain(dve, s_c)
            for b, rr in enumerate(ROWS):
                dve.wait_ge(s_g[b], 32)
                x = K.X[0:rr, b, :]
                for j in range(2):
                    do(nc.vector.scalar_tensor_tensor(out=x, in0=Y[0:rr, b, j, :], scalar=K.wts[0:rr, b, j:j + 1], in1=x, op0=ALU.mult, op1=ALU.add))


def attention_layout(K):
    at = A_XS
    K.QT, K.KTr = K.region(at, KT, TOK), K.region(at + KT * TOK, KT, TOK)
    K.VN = K.HN()
    at += 2 * KT * TOK
    K.a0 = at
    K.kv_early = at + KT * TOK + NB * D + 4 * KT * P
    K.kv_late = at
    K.s_pages = {n: [K.sem(f"pages_{n}{v}") for v in range(2)] for n in "kv"}
    K.ptab = K.sb("ptab", [1, DB * NPG], I32)
    K.sbb = K.sb("sbb", [P, NH])
    K.s_small = K.sem("attn_small")


def load_pages(K, sp, seq, v, base, name):
    pages = K.region(base, NPG, D)
    npool = K.d["cache_k"].shape[1]
    src = K.d["cache_" + name][0].rearrange("n r h c -> n r (h c)")
    for g in range(NPG):
        page = sp.value_load(K.ptab[0:1, bass.ds(seq * NPG + g, 1)], min_val=0, max_val=npool - 1)
        sp.dma_start(pages[:, g, :], src[page]).then_inc(K.s_pages[name][v], 16)


def stage_qkv(K):
    nc, d = K.nc, K.d
    s = {n: K.sem(f"qkv_{n}") for n in ("proj", "a", "v")}
    s_w = [K.sem(f"qkv_w{u}") for u in range(4)]
    HT = K.HT()
    at = K.a0
    VT = K.region(at, KT, TOK); at += KT * TOK
    KN = K.region(at, NB, D); at += NB * D
    wt = [K.region(at + u * KT * P, KT, P) for u in range(4)]; at += 4 * KT * P
    dst = [K.QT, K.KTr, VT]
    scale = [DH ** -0.5, 1.0, 1.0]
    wsrc = d["sb_w_qkv"][0].rearrange("(k p) (m c) -> m p k c", p=P, c=P)
    U = 4

    with nc.Block() as block:
        @block.sync
        def _(sp):
            sp.dma_start(K.ptab[:], d["page_table"].rearrange("s g -> (s g)").unsqueeze(0)).then_inc(K.s_small, 16)
            sp.dma_start(K.sbb[:], d["sb_logit_bias"].partition_broadcast(P)).then_inc(K.s_small, 16)
            with sp.Fori(0, 3 * KT // U) as it:
                for u in range(U):
                    sp.wait_ge(s["proj"], U * it + u + 1)
                    sp.dma_start(wt[u], wsrc[U * it + u]).then_inc(s_w[u], 16)
            sp.wait_ge(K.s_small, 32)
            load_pages(K, sp, 0, 0, K.kv_early, "k")
            load_pages(K, sp, 0, 0, K.kv_early + NPG * D, "v")

        @block.tensor
        def _(pe):
            pe.sem_inc(s["proj"], U)
            with pe.Fori(0, 3 * KT // U) as it:
                for u in range(U):
                    e = U * it + u
                    pe.wait_ge(s_w[u], 16 * it + 16)
                    pe.wait_ge(s["a"], e + 1)
                    pe.wait_ge(s["v"], e + 1)
                    for n in range(2):
                        for k in range(KT):
                            last = nc.tensor.matmul(K.ps[2 * u + n][:, 0:HALF], wt[u][:, k, :], HT[:, k, n * HALF:(n + 1) * HALF],
                                                    start=(k == 0), stop=(k == KT - 1))
                    last.then_inc(s["proj"], 1)

        @block.scalar
        def _(act):
            act.sem_inc(s["a"], U)
            for part in range(3):
                with act.Fori(0, KT // U) as it:
                    for u in range(U):
                        m = U * it + u
                        act.wait_ge(s["proj"], KT * part + m + U + 1)
                        K.settle(act)
                        nc.scalar.activation(dst[part][:, m, 0:HALF], K.ps[2 * u][:, 0:HALF], ACT.Copy, scale=scale[part]).then_inc(s["a"], 1)

        @block.vector
        def _(dve):
            dve.sem_inc(s["v"], U)
            for part in range(3):
                with dve.Fori(0, KT // U) as it:
                    for u in range(U):
                        m = U * it + u
                        dve.wait_ge(s["proj"], KT * part + m + U + 1)
                        nc.vector.tensor_scalar(dst[part][:, m, HALF:TOK], K.ps[2 * u + 1][:, 0:HALF], scale[part], None, ALU.mult).then_inc(s["v"], 1)

    s = {n: K.sem(f"kvrows_{n}") for n in ("turned", "a", "v", "out")}
    with nc.Block() as block:
        groups = [(src, b, h) for src in range(2) for b in range(NB) for h in range(2)]

        @block.tensor
        def _(pe):
            for t, (src, b, h) in enumerate(groups):
                r = ROWS[b]
                if t >= 8:
                    pe.wait_ge(s["av"[t % 2]], (t - 8) // 2 + 1)
                for q in range(4):
                    last = nc.tensor.transpose(K.ps[t % 8][0:r, q * P:(q + 1) * P], (K.KTr, VT)[src][:, 4 * h + q, b * P:b * P + r], K.ident[:])
                last.then_inc(s["turned"], 1)

        def rows_out(eng, mine, copy):
            for t, (src, b, h) in enumerate(groups):
                if t % 2 == mine:
                    r = ROWS[b]
                    eng.wait_ge(s["turned"], t + 1)
                    copy((KN, K.VN)[src][0:r, b, h * 512:(h + 1) * 512], K.ps[t % 8][0:r, :]).then_inc(s["av"[mine]], 1)

        @block.scalar
        def _(act):
            rows_out(act, 0, lambda o, i: nc.scalar.activation(o, i, ACT.Copy))

        @block.vector
        def _(dve):
            rows_out(dve, 1, nc.vector.tensor_copy)

        @block.sync
        def _(sp):
            for src, (buf, name) in enumerate(((KN, "k_rows"), (K.VN, "v_rows"))):
                sp.wait_ge(s["a"], NB * (src + 1))
                sp.wait_ge(s["v"], NB * (src + 1))
                sp.dma_start(d[name + "_p"][0, 0].rearrange("(b p) h c -> p b (h c)", p=P), buf[:, 0:4, :]).then_inc(s["out"], 16)
                sp.dma_start(d[name + "_s"][0].rearrange("s t h c -> (s t) (h c)"), buf[0:NS, 4, :]).then_inc(s["out"], 16)
            sp.wait_ge(s["out"], 64)


def stage_sample_attention(K):
    nc, d = K.nc, K.d
    names = ("mask", "maskT", "ready", "qb", "ka", "kd", "z", "az", "e", "l", "r", "sp", "spm", "scan", "t", "tt",
             "ea", "atr", "at", "av", "om", "sel", "o", "r2", "c")
    s = {n: K.sem(f"sample_{n}") for n in names}
    OT = K.HT()
    R = NH * DS
    NK = PAST + NS
    base = [K.kv_early, K.kv_late]
    kp = [K.region(b, NPG, D) for b in base]
    vp = [K.region(b + NPG * D, NPG, D) for b in base]
    at = K.kv_late + 2 * NPG * D
    KS = K.region(at, KT, NPG * P); at += KT * NPG * P
    kv_gap = at
    at = K.kv_early + 2 * NPG * D
    spaces = [[kv_gap, K.kv_early], [at, A_END]]

    def rows(*dims, r=P):
        n = 1
        for x in dims:
            n *= x
        space = [x for x in spaces if x[0] + n <= x[1]][0]
        v = K.region(space[0], *dims)[0:r]
        space[0] += n
        return v

    az, spb = (rows(NK, r=R) for _ in range(2))
    A = [rows(NK, r=R) for _ in range(2)]
    AT = [rows((NPG + 1) * R) for _ in range(2)]
    QW = KT * (R + 8)
    qb = [rows(QW) for _ in range(2)]
    neg, m01 = rows(DB, NS, r=R), rows(DB, NS, r=R)
    assert 2 * R == P
    one_hot = [rows(NH, DS) for _ in range(2)]
    sel, hot_h, bcol = rows(2, DS), rows(NH, r=R), rows(1, r=R)
    own_half = K.sb("own_head", [P, 2, D // 2])
    own = own_half[:, 0, :]
    Om = K.sb("own_rows", [P, D // 2])
    maskT = Om[:, 0:DB * R].rearrange("p (s c) -> p s c", s=DB)
    ones_row = K.ones[0:R, 0:1].to_broadcast([R, NK])
    z = K.psum[0:R, 1024:1024 + NK]
    znew = K.psum[0:R, 1024 + PAST:1024 + NK]
    TB = (0, 1, 4)
    O = K.ps[5]
    picked = K.ps[3][:, 64:64 + KT * DS]
    mm = nc.tensor.matmul

    def static_below(x, n):
        return isinstance(x, int) and x < n

    with nc.Block() as block:
        @block.sync
        def _(sp):
            def body(it, us):
                for u in us:
                    seq = 2 * it + u
                    if not static_below(seq, 2):
                        sp.wait_ge(s["t"], KT * (seq - 1))
                        K.settle(sp)
                    load_pages(K, sp, seq, u, base[u], "k")
                    if not static_below(seq, 2):
                        sp.wait_ge(s["av"], seq - 1)
                        K.settle(sp)
                    load_pages(K, sp, seq, u, base[u] + NPG * D, "v")
            body(0, (1,))
            with sp.Fori(1, DB // 2) as it:
                body(it, (0, 1))

        @block.gpsimd
        def _(pool):
            g = nc.gpsimd
            v4 = maskT.rearrange("p s (h t) -> p s h t", t=DS)
            g.memset(maskT, 1.0)
            g.memset(one_hot[0], 0.0)
            g.memset(one_hot[1], 0.0)
            g.memset(own_half[:], 1.0).then_inc(s["mask"], 1)
            pool.wait_ge(s["mask"], 1)
            g.affine_select(out=v4, in_=v4, compare_op=ALU.is_ge, fill=0.0, base=0,
                            pattern=[[-DS, DB], [0, NH], [0, DS]], channel_multiplier=1)
            for half in range(2):
                o3 = own_half[:, half, :].rearrange("r (h c) -> r h c", h=NH // 2)
                last = g.affine_select(out=o3, in_=o3, compare_op=ALU.is_ge, fill=0.0, base=-half * (R + R // 2),
                                       pattern=[[-DS, NH // 2], [0, DH]], channel_multiplier=1)
            last.then_inc(s["mask"], 1)
            pool.wait_ge(s["mask"], 2)
            g.affine_select(out=v4, in_=v4, compare_op=ALU.is_gt, fill=0.0, base=0,
                            pattern=[[DS, DB], [0, NH], [1, DS]], channel_multiplier=-1)
            for half in range(2):
                o3 = own_half[:, half, :].rearrange("r (h c) -> r h c", h=NH // 2)
                g.affine_select(out=o3, in_=o3, compare_op=ALU.is_ge, fill=0.0, base=DS - 1 + half * (R + R // 2),
                                pattern=[[DS, NH // 2], [0, DH]], channel_multiplier=-1)
            for half in range(2):
                last = g.affine_select(out=one_hot[half], in_=one_hot[half], compare_op=ALU.not_equal, fill=1.0, base=-R * half,
                                       pattern=[[-DS, NH], [-1, DS]], channel_multiplier=1)
            last.then_inc(s["mask"], 1)
            pool.wait_ge(s["mask"], 3)
            g.tensor_tensor(own, own, own_half[:, 1, :], ALU.add).then_inc(s["mask"], 1)

        @block.tensor
        def _(pe):
            def weights_turned(e, w):
                pe.wait_ge(s["ea"], e + 1)
                if not static_below(e, 1):
                    pe.wait_ge(s["at"], e)
                K.settle(pe)
                for g in range(NPG):
                    nc.tensor.transpose(K.ps[7][:, g * R:(g + 1) * R], A[w][:, g * P:(g + 1) * P], K.ident[0:R, 0:R])
                nc.tensor.transpose(K.ps[7][0:NS, NPG * R:(NPG + 1) * R], A[w][:, PAST:NK], K.ident[0:R, 0:R]).then_inc(s["atr"], 1)

            def pick(e):
                pe.wait_ge(s["om"], e + 1)
                for m in range(KT):
                    last = mm(picked[:, DS * m:DS * (m + 1)], Om[:, m % 4 * P:(m % 4 + 1) * P], sel[:, m // 4, :], start=True, stop=True)
                last.then_inc(s["sel"], 1)

            def values(e, w, it):
                pe.wait_ge(s["at"], e + 1)
                pe.wait_ge(K.s_pages["v"][w], NPG * 16 * (it + 1))
                if not static_below(e, 1):
                    pe.wait_ge(s["om"], e)
                for g in range(NPG + 1):
                    for n in range(2):
                        cols, out = slice(n * 512, (n + 1) * 512), O[R * n:R * (n + 1), :]
                        if g < NPG:
                            mm(out, AT[w][:, g * R:(g + 1) * R], vp[w][:, g, cols], start=(g == 0), stop=False)
                        else:
                            last = mm(out, AT[w][0:NS, NPG * R:(NPG + 1) * R], K.VN[0:NS, NB - 1, cols], start=False, stop=True)
                last.then_inc(s["av"], 1)

            def body(it):
                for v in range(2):
                    e = 2 * it + v
                    pe.wait_ge(K.s_pages["k"][v], NPG * 16 * (it + 1))
                    for m in range(KT):
                        m2, e2 = (m - 3, e) if m >= 3 else (m + 5, e - 1)
                        if not static_below(e2, 0):
                            pe.wait_ge(s["kd" if m2 % 2 else "ka"], 4 * e2 + m2 // 2 + 1)
                        for g in range(NPG):
                            last = nc.tensor.transpose(K.ps[TB[m % 3]][:, g * P:(g + 1) * P], kp[v][:, g, m * P:(m + 1) * P], K.ident[:])
                        last.then_inc(s["t"], 1)
                    if not static_below(e, 1):
                        weights_turned(e - 1, 1 - v)
                    if not static_below(e, 2):
                        pick(e - 2)
                    pe.wait_ge(s["qb"], e + 1)
                    pe.wait_ge(s["ka"], 4 * e + 4)
                    pe.wait_ge(s["kd"], 4 * e + 4)
                    if not static_below(e, 1):
                        pe.wait_ge(s["tt"], e)
                    for m in range(KT):
                        mm(z[:, 0:PAST], qb[v][:, m * R:(m + 1) * R], KS[:, m, :], start=(m == 0), stop=(m == KT - 1))
                    if not static_below(e, 2):
                        pe.wait_ge(s["o"], e - 1)
                    for m in range(KT):
                        last = mm(znew, qb[v][:, m * R:(m + 1) * R], K.KTr[:, m, SEQ:TOK], start=(m == 0), stop=(m == KT - 1))
                    last.then_inc(s["z"], 1)
                    if not static_below(e, 1):
                        values(e - 1, 1 - v, it if v else it - 1)

            pe.wait_ge(s["mask"], 4)
            for q in range(DB):
                last = nc.tensor.transpose(K.ps[7][0:R, q * NS:(q + 1) * NS], maskT[0:NS, q, :], K.ident[0:NS, 0:NS])
            last.then_inc(s["maskT"], 1)
            pe.wait_ge(s["ready"], 1)
            body(0)
            with pe.Fori(1, DB // 2) as it:
                body(it)
            weights_turned(DB - 1, 1)
            pick(DB - 2)
            values(DB - 1, 1, DB // 2 - 1)
            pe.wait_ge(s["o"], DB - 1)
            pick(DB - 1)

        def keys_out(eng, e, mine, copy):
            if not static_below(e, 1):
                eng.wait_ge(s["z"], e)
            for m in range(mine, KT, 2):
                eng.wait_ge(s["t"], KT * e + m + 1)
                copy(KS[:, m, :], K.ps[TB[m % 3]][:]).then_inc(s["kd" if mine else "ka"], 1)

        @block.scalar
        def _(act):
            def turned_out(e, w):
                act.wait_ge(s["atr"], e + 1)
                if not static_below(e, 2):
                    act.wait_ge(s["av"], e - 1)
                nc.scalar.activation(AT[w][:, 0:NPG * R], K.ps[7][:, 0:NPG * R], ACT.Copy)
                nc.scalar.activation(AT[w][0:NS, NPG * R:(NPG + 1) * R], K.ps[7][0:NS, NPG * R:(NPG + 1) * R], ACT.Copy).then_inc(s["at"], 1)

            def body(it):
                for v in range(2):
                    e = 2 * it + v
                    keys_out(act, e, 0, lambda a, b: nc.scalar.activation(a, b, ACT.Copy))
                    if not static_below(e, 1):
                        turned_out(e - 1, 1 - v)
                        act.wait_ge(s["sp"], e)
                    act.wait_ge(s["z"], e + 1)
                    nc.scalar.activation(az, z, ACT.Abs, bias=bcol).then_inc(s["az"], 1)
                    act.wait_ge(s["az"], e + 1)
                    nc.scalar.activation(az, az, ACT.Exp, scale=-1.0).then_inc(s["e"], 1)
                    act.wait_ge(s["e"], e + 1)
                    nc.scalar.activation(az, az, ACT.Ln, bias=1.0).then_inc(s["l"], 1)
                    act.wait_ge(s["tt"], e + 1)
                    nc.scalar.activation(A[v], A[v], ACT.Exp).then_inc(s["ea"], 1)

            body(0)
            with act.Fori(1, DB // 2) as it:
                body(it)
            turned_out(DB - 1, 1)

        @block.vector
        def _(dve):
            vec = nc.vector

            def own_features(e):
                dve.wait_ge(s["av"], e + 1)
                vec.tensor_tensor(Om[:], O, own, ALU.mult).then_inc(s["om"], 1)

            def heads_out(e):
                dve.wait_ge(s["sel"], e + 1)
                vec.tensor_copy(OT[:, :, bass.ds(SEQ + DS * e, DS)], picked.rearrange("p (m t) -> p m t", m=KT)).then_inc(s["o"], 1)

            def body(it):
                for v in range(2):
                    e = 2 * it + v
                    if not static_below(e, 2):
                        dve.wait_ge(s["z"], e - 1)
                    diag = qb[v].rearrange("p (m c) -> p m c", c=R + 8)
                    for q in range(2):
                        last = vec.tensor_copy(diag[64 * q:64 * q + 64, :, DS * q:DS * q + DS], K.QT[64 * q:64 * q + 64, :, bass.ds(SEQ + DS * e, DS)])
                    last.then_inc(s["qb"], 1)
                    keys_out(dve, e, 1, vec.tensor_copy)
                    if not static_below(e, 2):
                        heads_out(e - 2)
                    dve.wait_ge(s["az"], e + 1)
                    vec.tensor_scalar(spb, z, bcol, 0.0, ALU.add, ALU.max).then_inc(s["r"], 1)
                    dve.wait_ge(s["r"], e + 1)
                    dve.wait_ge(s["l"], e + 1)
                    vec.tensor_tensor(spb, spb, az, ALU.add).then_inc(s["sp"], 1)
                    dve.wait_ge(s["sp"], e + 1)
                    new = spb[:, PAST:NK]
                    vec.tensor_tensor(new, new, m01[:, bass.ds(e, 1), :].rearrange("p a c -> p (a c)"), ALU.mult).then_inc(s["spm"], 1)
                    dve.wait_ge(s["spm"], e + 1)
                    vec.tensor_tensor_scan(spb[:, ::-1], ones_row, spb[:, ::-1], 0.0, ALU.mult, ALU.add).then_inc(s["scan"], 1)
                    dve.wait_ge(s["scan"], e + 1)
                    if not static_below(e, 2):
                        dve.wait_ge(s["atr"], e - 1)
                    vec.scalar_tensor_tensor(out=A[v], in0=z, scalar=bcol, in1=spb, op0=ALU.add, op1=ALU.subtract).then_inc(s["r2"], 1)
                    dve.wait_ge(s["r2"], e + 1)
                    new = A[v][:, PAST:NK]
                    vec.tensor_tensor(new, new, neg[:, bass.ds(e, 1), :].rearrange("p a c -> p (a c)"), ALU.add).then_inc(s["tt"], 1)
                    if not static_below(e, 1):
                        own_features(e - 1)

            do = Chain(dve, s["c"])
            vec.memset(qb[0], 0.0)
            vec.memset(qb[1], 0.0)
            dve.wait_ge(s["mask"], 4)
            for half in range(2):
                do(vec.tensor_reduce(sel[:, half, :].unsqueeze(2), one_hot[half].rearrange("p h t -> p t h"), AX.X, ALU.add))
            do(vec.tensor_reduce(hot_h.unsqueeze(2), one_hot[0][0:R], AX.X, ALU.add))
            do(vec.tensor_tensor(hot_h, hot_h, K.sbb[0:R, :], ALU.mult))
            do(vec.tensor_reduce(bcol, hot_h, AX.X, ALU.add))
            dve.wait_ge(s["maskT"], 1)
            do(vec.tensor_copy(m01.rearrange("p s k -> p (s k)"), K.ps[7][0:R, 0:DB * NS]))
            do(vec.tensor_scalar(neg, m01, -1.0, -NEG, ALU.add, ALU.mult))
            dve.sem_inc(s["ready"], 1)
            body(0)
            with dve.Fori(1, DB // 2) as it:
                body(it)
            heads_out(DB - 2)
            own_features(DB - 1)
            heads_out(DB - 1)


def stage_prompt_attention(K):
    nc, d = K.nc, K.d
    names = ("qk", "v", "z", "az", "r", "e", "l", "sp", "spm", "cum", "ea", "am", "av", "o")
    s = {n: K.sem(f"prompt_{n}") for n in names}
    OT = K.HT()
    nkb = SEQ // P
    off, width = [0, 512, 1024, 896], [SEQ - P * kb for kb in range(4)]
    NC = sum(width)
    at = K.a0
    az = [K.region(at + v * NC, NC) for v in range(2)]; at += 2 * NC
    sp_ = [K.region(at + v * NC, NC) for v in range(2)]; at += 2 * NC
    A = [K.region(at + v * NC, NC) for v in range(2)]; at += 2 * NC
    qs = [K.region(at + v * SEQ, SEQ) for v in range(2)]; at += 2 * SEQ
    ks = [K.region(at + v * SEQ, SEQ) for v in range(2)]; at += 2 * SEQ
    vs = [K.region(at + v * SEQ, nkb, P) for v in range(2)]; at += 2 * SEQ
    assert at <= K.kv_early
    K.wo = K.region(K.kv_early, KT, D)
    K.s_wo = K.sem("wo")
    z = [K.psum[:, 1536 * v:1536 * v + NC] for v in range(2)]
    mm = nc.tensor.matmul
    iters = KT // 2

    def static_below(x, n):
        return isinstance(x, int) and x < n

    with nc.Block() as block:
        @block.sync
        def _(sp):
            sp.dma_start(K.wo, d["sb_w_o"][0].rearrange("(k p) c -> p k c", p=P)).then_inc(K.s_wo, 16)

        def heads(body):
            def four(it):
                for w in range(4):
                    body(2 * it + w // 2, w // 2, 4 * it + w, w % 2)
            return four

        def run(eng, body):
            four = heads(body)
            four(0)
            with eng.Fori(1, iters) as it:
                four(it)

        @block.tensor
        def _(pe):
            def sums(e, v):
                pe.wait_ge(s["spm"], e + 1)
                for kb in range(nkb):
                    last = mm(z[v][:, off[kb]:off[kb] + width[kb]], K.negtri[:], sp_[v][:, off[kb]:off[kb] + width[kb]], start=False, stop=(kb == nkb - 1), skip_group_check=True)
                    for k2 in range(kb + 1, nkb):
                        lo = off[kb] + P * (k2 - kb)
                        mm(z[v][:, lo:lo + width[k2]], K.negones[:], sp_[v][:, off[k2]:off[k2] + width[k2]], start=False, stop=False, skip_group_check=True)
                return last

            def values(m, pv, e, v):
                pe.wait_ge(s["am"], e + 1)
                if v == 0:
                    pe.wait_ge(s["v"], m + 1)
                    if not static_below(m, 2):
                        pe.wait_ge(s["o"], m - 1)
                out = K.ps[6 + pv][64 * v:64 * v + 64, :]
                for kb in range(nkb):
                    last = mm(out[:, P * kb:SEQ], vs[pv][:, kb, 64 * v:64 * v + 64], A[v][:, off[kb]:off[kb] + width[kb]],
                              start=(kb == 0), stop=(kb == nkb - 1), skip_group_check=True)
                last.then_inc(s["av"], 1)

            def body(m, pv, e, v):
                if v == 0:
                    pe.wait_ge(s["qk"], m + 1)
                if not static_below(e, 2):
                    pe.wait_ge(s["ea"], e - 1)
                half = slice(64 * v, 64 * v + 64)
                for kb in (0, 1, 3, 2):
                    last = mm(z[v][:, off[kb]:off[kb] + width[kb]], ks[pv][half, P * kb:P * kb + P], qs[pv][half, P * kb:SEQ],
                              start=(kb != 3), stop=(kb == 2), skip_group_check=True)
                last.then_inc(s["z"], 1)
                if not static_below(e, 1):
                    sums(e - 1, 1 - v).then_inc(s["cum"], 1)
                if not static_below(e, 2):
                    values(m - 1, 1 - pv, e - 2, v)

            run(pe, body)
            sums(NH - 1, 1).then_inc(s["cum"], 1)
            values(KT - 1, 1, NH - 2, 0)
            values(KT - 1, 1, NH - 1, 1)

        @block.scalar
        def _(act):
            def weights(e, v):
                act.wait_ge(s["cum"], e + 1)
                if not static_below(e, 2):
                    act.wait_ge(s["av"], e - 1)
                K.settle(act)
                nc.scalar.activation(A[v], z[v], ACT.Exp, bias=K.sbb[:, bass.ds(e, 1)]).then_inc(s["ea"], 1)

            def body(m, pv, e, v):
                act.wait_ge(s["z"], e + 1)
                if not static_below(e, 2):
                    act.wait_ge(s["sp"], e - 1)
                K.settle(act)
                nc.scalar.activation(az[v], z[v], ACT.Abs, bias=K.sbb[:, bass.ds(e, 1)]).then_inc(s["az"], 1)
                act.wait_ge(s["az"], e + 1)
                nc.scalar.activation(az[v], az[v], ACT.Exp, scale=-1.0).then_inc(s["e"], 1)
                act.wait_ge(s["e"], e + 1)
                nc.scalar.activation(az[v], az[v], ACT.Ln, bias=1.0).then_inc(s["l"], 1)
                if not static_below(e, 1):
                    weights(e - 1, 1 - v)

            run(act, body)
            weights(NH - 1, 1)

        @block.vector
        def _(dve):
            def pair_out(m, pv):
                dve.wait_ge(s["av"], 2 * m + 2)
                nc.vector.tensor_copy(OT[:, bass.ds(m, 1), 0:SEQ].rearrange("p a c -> p (a c)"), K.ps[6 + pv][:]).then_inc(s["o"], 1)

            def stage_qk(m, pv):
                nc.vector.tensor_copy(qs[pv], K.QT[:, bass.ds(m, 1), 0:SEQ].rearrange("p a c -> p (a c)"))
                nc.vector.tensor_copy(ks[pv], K.KTr[:, bass.ds(m, 1), 0:SEQ].rearrange("p a c -> p (a c)")).then_inc(s["qk"], 1)

            def stage_v(m, pv):
                if not static_below(m, 2):
                    dve.wait_ge(s["av"], 2 * m - 2)
                nc.vector.tensor_copy(vs[pv], K.VN[:, 0:nkb, bass.ds(m * P, P)]).then_inc(s["v"], 1)

            def body(m, pv, e, v):
                dve.wait_ge(s["az"], e + 1)
                if not static_below(e, 2):
                    dve.wait_ge(s["cum"], e - 1)
                nc.vector.tensor_scalar(sp_[v], z[v], K.sbb[:, bass.ds(e, 1)], 0.0, ALU.add, ALU.max).then_inc(s["r"], 1)
                if v == 1:
                    stage_v(m, pv)
                elif not (isinstance(m, int) and m == KT - 1):
                    stage_qk(m + 1, 1 - pv)
                dve.wait_ge(s["r"], e + 1)
                dve.wait_ge(s["l"], e + 1)
                nc.vector.tensor_tensor(sp_[v], sp_[v], az[v], ALU.add).then_inc(s["sp"], 1)
                if v == 1 and not static_below(m, 1):
                    pair_out(m - 1, 1 - pv)

            stage_qk(0, 0)
            four = heads(body)
            four(0)
            with dve.Fori(1, iters - 1) as it:
                four(it)
            four(iters - 1)
            pair_out(KT - 1, 1)

        @block.gpsimd
        def _(pool):
            def diagonals(t):
                K.settle(pool)
                for kb in range(nkb):
                    x = t[:, off[kb]:off[kb] + P]
                    last = nc.gpsimd.affine_select(out=x, in_=x, compare_op=ALU.is_gt, fill=0.0, base=0, pattern=[[1, P]], channel_multiplier=-1)
                return last

            def masked_weights(e, v):
                pool.wait_ge(s["ea"], e + 1)
                diagonals(A[v]).then_inc(s["am"], 1)

            def body(m, pv, e, v):
                pool.wait_ge(s["sp"], e + 1)
                diagonals(sp_[v]).then_inc(s["spm"], 1)
                if not static_below(e, 1):
                    masked_weights(e - 1, 1 - v)

            run(pool, body)
            masked_weights(NH - 1, 1)


def stage_project(K, tag, src, w, s_w):
    nc = K.nc
    s = {n: K.sem(f"{tag}_{n}") for n in ("y", "added")}
    with nc.Block() as block:
        @block.tensor
        def _(pe):
            pe.wait_ge(s_w, 16)
            for b, r in enumerate(ROWS):
                for n in range(2):
                    g = 2 * b + n
                    if g >= 8:
                        pe.wait_ge(s["added"], g - 7)
                    for k in range(KT):
                        last = nc.tensor.matmul(K.ps[g % 8][0:r, :], src[:, k, b * P:b * P + r], w[:, k, n * 512:(n + 1) * 512],
                                                start=(k == 0), stop=(k == KT - 1))
                    last.then_inc(s["y"], 1)

        @block.scalar
        def _(act):
            square_sums(K, act, s["added"], 2, [K.region(A_HN + D * b, D) for b in range(NB)])

        @block.vector
        def _(dve):
            for b, r in enumerate(ROWS):
                for n in range(2):
                    g = 2 * b + n
                    dve.wait_ge(s["y"], g + 1)
                    x = K.X[0:r, b, n * 512:(n + 1) * 512]
                    nc.vector.tensor_tensor(x, x, K.ps[g % 8][0:r, :], ALU.add).then_inc(s["added"], 1)


def stage_final(K):
    nc, d = K.nc, K.d
    s = {n: K.sem(f"final_{n}") for n in ("g", "ms", "root", "rstd", "y", "out")}
    Y, g = K.HN(), K.region(A_HT, D)
    with nc.Block() as block:
        @block.sync
        def _(sp):
            sp.dma_start(g, d["norm_final"].partition_broadcast(P)).then_inc(s["g"], 16)
            for b, r in enumerate(ROWS):
                sp.wait_ge(s["y"], b + 1)
                dst = d["y_prompt"][0, b * P:(b + 1) * P, :] if b < NB - 1 else d["y_sample"].rearrange("s t c -> (s t) c")
                sp.dma_start(dst, Y[0:r, b, :]).then_inc(s["out"], 16)
            sp.wait_ge(s["out"], 16 * NB)

        @block.scalar
        def _(act):
            act.wait_ge(s["ms"], 1)
            nc.scalar.activation(K.rstd[:], K.ss[:], ACT.Sqrt).then_inc(s["root"], 1)

        @block.vector
        def _(dve):
            nc.vector.tensor_scalar(K.ss[:], K.ss[:], 1.0 / D, NORM_EPS, ALU.mult, ALU.add).then_inc(s["ms"], 1)
            dve.wait_ge(s["root"], 1)
            nc.vector.reciprocal(K.rstd[:], K.rstd[:]).then_inc(s["rstd"], 1)
            dve.wait_ge(s["rstd"], 1)
            dve.wait_ge(s["g"], 16)
            for b, r in enumerate(ROWS):
                nc.vector.scalar_tensor_tensor(out=Y[0:r, b, :], in0=K.X[0:r, b, :], scalar=K.rstd[0:r, b:b + 1], in1=g[0:r],
                                               op0=ALU.mult, op1=ALU.mult).then_inc(s["y"], 1)


def build(nc, dram, stages):
    with ExitStack() as ctx:
        K = Kernel(nc, ctx, dram)
        for st in stages(K):
            st()


def program(K):
    return [
        lambda: stage_setup(K),
        lambda: stage_norm(K, "mix0", V_MIX),
        lambda: stage_conv_in(K),
        lambda: stage_conv_out(K),
        lambda: stage_norm(K, "ffn0", V_FFN),
        lambda: stage_route(K, 0),
        lambda: stage_moe(K, 0),
        K.recycle,
        lambda: attention_layout(K),
        lambda: stage_norm(K, "mix1", V_MIX + 1),
        lambda: stage_qkv(K),
        lambda: stage_sample_attention(K),
        lambda: stage_prompt_attention(K),
        lambda: stage_project(K, "wo", K.HT(), K.wo, K.s_wo),
        lambda: stage_norm(K, "ffn1", V_FFN + 1),
        lambda: stage_route(K, 1),
        lambda: stage_moe(K, 1),
        lambda: stage_final(K),
    ]


INPUTS = ["x_prompt", "x_sample", "state_conv", "cache_k", "cache_v", "page_table", "norm_mix", "norm_ffn", "norm_final",
          "conv_w_pw1", "conv_b_pw1", "conv_w_dw", "conv_b_dw", "conv_ln_g", "conv_ln_b", "conv_w_pw2", "conv_b_pw2",
          "sb_w_qkv", "sb_w_o", "sb_logit_bias", "moe_w_coarse", "moe_b_coarse", "moe_w_fine", "moe_b_fine",
          "moe_w_gate", "moe_w_up", "moe_w_down"]
OUTPUTS = {
    "y_prompt": (1, SEQ, D), "y_sample": (DB, DS, D), "conv_state_p": (1, 1, HIST, D), "conv_state_s": (1, DB, HIST, D),
    "k_rows_p": (1, 1, SEQ, NH, DH), "v_rows_p": (1, 1, SEQ, NH, DH),
    "k_rows_s": (1, DB, DS, NH, DH), "v_rows_s": (1, DB, DS, NH, DH),
}


def kernel(**inputs):
    import numpy as np
    import concourse.bacc as bacc
    from concourse.bass_utils import run_bass_kernel_spmd

    nc = bacc.Bacc("TRN2", target_bir_lowering=False, num_devices=1)
    dram, arrays = {}, {}
    for name in INPUTS:
        a = np.ascontiguousarray(inputs[name])
        arrays[name] = a
        dram[name] = nc.dram_tensor(name, a.shape, mybir.dt.from_np(a.dtype), kind="ExternalInput").ap()
    for name, shape in OUTPUTS.items():
        dram[name] = nc.dram_tensor(name, shape, F32, kind="ExternalOutput").ap()
    build(nc, dram, program)
    r = run_bass_kernel_spmd(nc, [arrays], core_ids=[0])
    return tuple(r.results[0][name] for name in OUTPUTS)
```
